# Optimizing a Trainium2 kernel written in Bass

```python
import math
import jax, jax.numpy as jnp
from jax import lax
import numpy as np

D_MODEL = 1024
BATCH = 1
SEQ = 512
DEPTH = 1

ATTN_GROUPS = ((128, 1), (512, 4), (2048, 16))
N_GROUPS = len(ATTN_GROUPS)
HEADS_PER_GROUP = 8
HEAD_DIM = 64
ATTN_HEADS = N_GROUPS * HEADS_PER_GROUP
ATTN_WIDTH = ATTN_HEADS * HEAD_DIM
ATTN_OUT = HEADS_PER_GROUP * HEAD_DIM
ATTN_BLOCK = 64
REL_BUCKETS = 32
REL_MAX_DIST = 1024
HGRN_EXPAND = 128
HGRN_HEADS = D_MODEL // HGRN_EXPAND
HGRN_KDIM = HGRN_EXPAND
HGRN_VDIM = D_MODEL // HGRN_HEADS
HGRN_WIDTH = HGRN_HEADS * HGRN_KDIM
HGRN_CHUNK = 64
D_FF = 2816
N_BRANCHES = 2
EPS = 1e-6
NEG_INF = -1e30

IN_SPLITS = (ATTN_WIDTH,) * 3 + (HGRN_WIDTH,) * 5 + (D_MODEL,) * N_BRANCHES
IN_WIDTH = sum(IN_SPLITS)
IN_OFFSETS = tuple(int(v) for v in np.cumsum(IN_SPLITS)[:-1])

kernel_name = 'hybrid_dilated_attn_hgrn2_macaron_block'

def rmsnorm(x, g):
    xf = x.astype(jnp.float32)
    y = xf * lax.rsqrt(jnp.mean(xf * xf, axis=-1, keepdims=True) + EPS)
    return (y * g.astype(jnp.float32)).astype(x.dtype)

def swiglu(x, w_in, w_out):
    gate, up = jnp.split(x @ w_in, 2, axis=-1)
    return (jax.nn.silu(gate) * up) @ w_out

def t5_bucket(rel):
    nb = REL_BUCKETS // 2
    max_exact = nb // 2
    ret = jnp.where(rel > 0, nb, 0)
    n = jnp.abs(rel)
    nf = jnp.maximum(n, 1).astype(jnp.float32)
    large = max_exact + (jnp.log(nf / max_exact) / math.log(REL_MAX_DIST / max_exact)
                         * (nb - max_exact)).astype(jnp.int32)
    large = jnp.minimum(large, nb - 1)
    return ret + jnp.where(n < max_exact, n, large)

def dilated_group_attention(q, k, v, bias_table, window, dilation):
    B, S, Hg, hd = q.shape
    half = window // (2 * dilation)
    L = S // dilation
    nb = -(-L // ATTN_BLOCK)
    Lp = nb * ATTN_BLOCK

    def to_sub(t):
        return t.reshape(B, L, dilation, Hg, hd).transpose(0, 2, 3, 1, 4)

    qs = jnp.pad(to_sub(q), ((0, 0),) * 3 + ((0, Lp - L), (0, 0)))
    pad_kv = ((0, 0),) * 3 + ((ATTN_BLOCK, Lp - L + ATTN_BLOCK), (0, 0))
    ks = jnp.pad(to_sub(k), pad_kv)
    vs = jnp.pad(to_sub(v), pad_kv)
    qb = qs.reshape(B, dilation, Hg, nb, ATTN_BLOCK, hd)

    def band(t):
        tb = t.reshape(B, dilation, Hg, nb + 2, ATTN_BLOCK, hd)
        return jnp.concatenate([tb[:, :, :, :nb], tb[:, :, :, 1:nb + 1], tb[:, :, :, 2:]], axis=-2)

    kb, vb = band(ks), band(vs)
    t_idx = jnp.arange(ATTN_BLOCK)[:, None]
    c_idx = jnp.arange(3 * ATTN_BLOCK)[None, :]
    delta = c_idx - ATTN_BLOCK - t_idx
    key_sub = jnp.arange(nb)[:, None, None] * ATTN_BLOCK + c_idx[None] - ATTN_BLOCK
    valid = (jnp.abs(delta) <= half)[None] & (key_sub >= 0) & (key_sub < L)
    bias = jnp.moveaxis(bias_table.astype(jnp.float32)[t5_bucket(delta * dilation)], -1, 0)

    s = jnp.einsum('bdhnqe,bdhnke->bdhnqk', qb, kb).astype(jnp.float32) * (HEAD_DIM ** -0.5)
    s = s + bias[None, None, :, None]
    s = jnp.where(valid[None, None, None], s, NEG_INF)
    lse = jax.nn.logsumexp(s, axis=-1)
    p = jnp.exp(s - lse[..., None])
    o = jnp.einsum('bdhnqk,bdhnke->bdhnqe', p.astype(v.dtype), vb)
    o = o.reshape(B, dilation, Hg, Lp, hd)[:, :, :, :L]
    lse = lse.reshape(B, dilation, Hg, Lp)[..., :L]
    o = o.transpose(0, 3, 1, 2, 4).reshape(B, S, Hg, hd)
    lse = lse.transpose(0, 3, 1, 2).reshape(B, S, Hg)
    return o, lse

def hgrn2_chunk_scan(q, k, v, logf):
    B, S, H, K = q.shape
    V = v.shape[-1]
    C = HGRN_CHUNK
    N = S // C

    def r(t):
        return t.reshape(B, N, C, H, t.shape[-1]).transpose(0, 3, 1, 2, 4)

    q, k, v, logf = r(q), r(k), r(v), r(logf)
    b = jnp.cumsum(logf, axis=3)
    ref = b[:, :, :, C // 2:C // 2 + 1]
    a = jnp.einsum('bhnck,bhnsk->bhncs', q * jnp.exp(b - ref), k * jnp.exp(ref - b))
    tri = jnp.tril(jnp.ones((C, C), dtype=bool))
    a = jnp.where(tri, a, 0.0)
    o_intra = jnp.einsum('bhncs,bhnsv->bhncv', a, v)
    b_last = b[:, :, :, -1:]
    u = jnp.einsum('bhnck,bhncv->bhnkv', k * jnp.exp(b_last - b), v)
    decay = jnp.exp(b_last[:, :, :, 0])

    def step(state, inp):
        d, du = inp
        return d[..., None] * state + du, state

    s0 = jnp.zeros((B, H, K, V), jnp.float32)
    _, s_start = lax.scan(step, s0, (decay.transpose(2, 0, 1, 3), u.transpose(2, 0, 1, 3, 4)))
    s_start = s_start.transpose(1, 2, 0, 3, 4)
    o_inter = jnp.einsum('bhnck,bhnkv->bhncv', q * jnp.exp(b), s_start)
    o = o_intra + o_inter
    return o.transpose(0, 2, 3, 1, 4).reshape(B, S, H, V)

def hgrn2_bidirectional(qz, fz_f, fz_b, iz, gz, lb_f, lb_b, norm_w):
    B, S, _ = qz.shape
    shp_k = (B, S, HGRN_HEADS, HGRN_KDIM)
    q = jax.nn.silu(qz.astype(jnp.float32)).reshape(shp_k)
    v = iz.astype(jnp.float32).reshape(B, S, HGRN_HEADS, HGRN_VDIM)

    def gates(fz, lb):
        f = lb.astype(jnp.float32) + (1.0 - lb.astype(jnp.float32)) * jax.nn.sigmoid(fz.astype(jnp.float32))
        return (1.0 - f).reshape(shp_k), jnp.log(f).reshape(shp_k)

    k_f, logf_f = gates(fz_f, lb_f)
    k_b, logf_b = gates(fz_b, lb_b)
    o_fwd = hgrn2_chunk_scan(q, k_f, v, logf_f)
    flip = lambda t: jnp.flip(t, axis=1)
    o_bwd = flip(hgrn2_chunk_scan(flip(q), flip(k_b), flip(v), flip(logf_b)))
    o = o_fwd + o_bwd
    o = o * lax.rsqrt(jnp.mean(o * o, axis=-1, keepdims=True) + EPS) * norm_w.astype(jnp.float32)
    o = o * jax.nn.silu(gz.astype(jnp.float32).reshape(B, S, HGRN_HEADS, HGRN_VDIM))
    return o.reshape(B, S, HGRN_HEADS * HGRN_VDIM).astype(qz.dtype)

def hybrid_mixer(h, w_in, rel_bias, lb_f, lb_b, hgrn_norm, w_proj_attn, w_proj_hgrn, w_out):
    B, S, _ = h.shape
    z = h @ w_in
    qa, ka, va, qh, fz_f, fz_b, ih, gh, gate_a, gate_h = jnp.split(z, IN_OFFSETS, axis=-1)

    shp = (B, S, N_GROUPS, HEADS_PER_GROUP, HEAD_DIM)
    qa, ka, va = qa.reshape(shp), ka.reshape(shp), va.reshape(shp)
    bias = rel_bias.reshape(REL_BUCKETS, N_GROUPS, HEADS_PER_GROUP)
    outs, lses = [], []
    for g, (window, dil) in enumerate(ATTN_GROUPS):
        o, lse = dilated_group_attention(qa[:, :, g], ka[:, :, g], va[:, :, g], bias[:, g], window, dil)
        outs.append(o)
        lses.append(lse)
    alpha = jax.nn.softmax(jnp.stack(lses, axis=0), axis=0)
    y_a = jnp.einsum('gbsh,gbshe->bshe', alpha, jnp.stack(outs, axis=0).astype(jnp.float32))
    y_a = y_a.reshape(B, S, ATTN_OUT).astype(h.dtype)

    y_h = hgrn2_bidirectional(qh, fz_f, fz_b, ih, gh, lb_f, lb_b, hgrn_norm)

    y = jax.nn.sigmoid(gate_a) * (y_a @ w_proj_attn) + jax.nn.sigmoid(gate_h) * (y_h @ w_proj_hgrn)
    return y @ w_out

def setup_inputs(seed: int = 0) -> dict:
    key = jax.random.key(seed)
    ks = jax.random.split(key, 18)
    f32 = jnp.float32

    def w(k, shape, fan_in):
        return jax.random.normal(k, shape, f32) * fan_in ** -0.5

    def gain(k, shape):
        return 1.0 + 0.02 * jax.random.normal(k, shape, f32)

    L = DEPTH
    return {
        'x': jax.random.normal(ks[0], (BATCH, SEQ, D_MODEL), f32),
        'ffn1_pre_norm': gain(ks[1], (L, D_MODEL)),
        'w_ffn1_in': w(ks[2], (L, D_MODEL, 2 * D_FF), D_MODEL),
        'w_ffn1_out': w(ks[3], (L, D_FF, D_MODEL), D_FF),
        'ffn1_post_norm': gain(ks[4], (L, D_MODEL)),
        'mix_pre_norm': gain(ks[5], (L, D_MODEL)),
        'w_in': w(ks[6], (L, D_MODEL, IN_WIDTH), D_MODEL),
        'rel_bias': 0.2 * jax.random.normal(ks[7], (REL_BUCKETS, ATTN_HEADS), f32),
        'hgrn_lb': 0.5 * jax.random.normal(ks[8], (2, DEPTH + 1, HGRN_WIDTH), f32),
        'hgrn_norm': gain(ks[9], (L, HGRN_VDIM)),
        'w_proj_attn': w(ks[10], (L, ATTN_OUT, D_MODEL), ATTN_OUT),
        'w_proj_hgrn': w(ks[11], (L, HGRN_HEADS * HGRN_VDIM, D_MODEL), HGRN_HEADS * HGRN_VDIM),
        'w_out': w(ks[12], (L, D_MODEL, D_MODEL), D_MODEL),
        'mix_post_norm': gain(ks[13], (L, D_MODEL)),
        'ffn2_pre_norm': gain(ks[14], (L, D_MODEL)),
        'w_ffn2_in': w(ks[15], (L, D_MODEL, 2 * D_FF), D_MODEL),
        'w_ffn2_out': w(ks[16], (L, D_FF, D_MODEL), D_FF),
        'ffn2_post_norm': gain(ks[17], (L, D_MODEL)),
    }

def reference(x, ffn1_pre_norm, w_ffn1_in, w_ffn1_out, ffn1_post_norm, mix_pre_norm, w_in,
              rel_bias, hgrn_lb, hgrn_norm, w_proj_attn, w_proj_hgrn, w_out, mix_post_norm,
              ffn2_pre_norm, w_ffn2_in, w_ffn2_out, ffn2_post_norm):
    lb_all = jnp.cumsum(jax.nn.softmax(hgrn_lb.astype(jnp.float32), axis=1), axis=1)
    for l in range(DEPTH):
        h = rmsnorm(x, ffn1_pre_norm[l])
        x = x + 0.5 * rmsnorm(swiglu(h, w_ffn1_in[l], w_ffn1_out[l]), ffn1_post_norm[l])

        h = rmsnorm(x, mix_pre_norm[l])
        y = hybrid_mixer(h, w_in[l], rel_bias, lb_all[0, l], lb_all[1, l], hgrn_norm[l],
                         w_proj_attn[l], w_proj_hgrn[l], w_out[l])
        x = x + rmsnorm(y, mix_post_norm[l])

        h = rmsnorm(x, ffn2_pre_norm[l])
        x = x + 0.5 * rmsnorm(swiglu(h, w_ffn2_in[l], w_ffn2_out[l]), ffn2_post_norm[l])
    return x


_drawn_inputs = setup_inputs


def setup_inputs(seed=0):
    import zlib

    import numpy as np

    out = dict(_drawn_inputs(seed))
    spreads = {}
    factors = {'ffn1_pre_norm': 3.087,
     'ffn1_post_norm': 4.851,
     'rel_bias': 2.685,
     'hgrn_norm': 3.65,
     'mix_post_norm': 10.773,
     'ffn2_pre_norm': 19.587,
     'ffn2_post_norm': 35.401}
    for name, (base, spread) in spreads.items():
        noise = np.random.default_rng([zlib.crc32(name.encode()), seed]).standard_normal(out[name].shape)
        drawn = base * np.exp(spread * noise) if base else spread * noise
        out[name] = __import__('jax').numpy.asarray(drawn.astype(out[name].dtype))
    for name, factor in factors.items():
        out[name] = (out[name] * factor).astype(out[name].dtype)
    return out
```

```python
import math
from contextlib import ExitStack

import numpy as np

import concourse.bass as bass
from concourse import mybir

ALU = mybir.AluOpType
ACT = mybir.ActivationFunctionType
AXIS_X = mybir.AxisListType.X
F32 = mybir.dt.float32
F32R = mybir.dt.float32r
U32 = mybir.dt.uint32

P = 128
D = 1024
KT = D // P
S = 512
FF = 2816
FT = FF // P
BLK = 1024
N_GROUPS, N_HEADS, HD = 3, 8, 64
PAIRS_H = N_HEADS // 2
R = 4
U = S // R
HALF = 64
DILATIONS = (1, 4, 16)
BUCKETS = 32
NEG_INF = -1e30
N_TAB = 2 * R - 1 + 2
VEC = 2 * U
GH_HEADS = 8
C = 64
NC_CH = S // C
TT = S // P
EPS = 1e-6

STAGES = (("ffn1_in", FT), ("ffn1_out", FT // 2), ("v", 2 * N_GROUPS), ("qk", N_GROUPS * PAIRS_H),
          ("gate_a", 6), ("ih", 4), ("hgrn", 2 * GH_HEADS), ("gate_h", KT), ("w_out", KT // 2),
          ("ffn3_in", FT), ("ffn3_out", FT // 2))
FIRST = {}
_n = 0
for _name, _count in STAGES:
    FIRST[_name] = _n
    _n += _count
N_PAIRS = _n


def bias_buckets():
    hot = np.zeros((BUCKETS + 1, N_TAB, VEC), np.float32)
    nb = BUCKETS // 2
    exact = nb // 2
    for c in range(N_TAB):
        for m in range(VEC):
            du = m - (U - 1)
            if c < 2 * R - 1:
                delta, dil, ok = R * du + c - (R - 1), DILATIONS[0], True
            elif c == 2 * R - 1:
                delta, dil, ok = du, DILATIONS[1], True
            else:
                delta, dil, ok = du // R, DILATIONS[2], du % R == 0
            if not ok or abs(delta) > HALF:
                hot[BUCKETS, c, m] = 1.0
                continue
            rel = delta * dil
            n = abs(rel)
            large = exact + int(np.float32(np.log(np.float32(max(n, 1)) / np.float32(exact)))
                                / np.float32(math.log(1024 / exact)) * np.float32(nb - exact))
            hot[(nb if rel > 0 else 0) + (n if n < exact else min(large, nb - 1)), c, m] = 1.0
    return hot.reshape(BUCKETS + 1, N_TAB * VEC)


def constants():
    s, c = np.arange(P)[:, None], np.arange(P)[None, :]
    same = s // C == c // C
    t = np.arange(S)[None, :] * np.ones((P, 1), int)
    parts = [s == c, same & (s <= c), same & (s >= c), t % C != 0, t % C != C - 1]
    return np.concatenate([x.astype(np.float32) for x in parts], axis=1)


def build(nc, wstream, x_t, params, rel_bias, onehot, consts, out_t):
    with ExitStack() as ctx:
        at = [(nc.sbuf_base + 63) // 64 * 64]

        def place(name, shape, dtype=F32):
            size = 4 * int(np.prod(shape[1:]))
            t = nc.alloc_sbuf_tensor_at(name, shape, dtype, offset=at[0])
            at[0] += (size + 31) // 32 * 32
            assert at[0] <= nc.sbuf_usable_end, (name, at[0])
            return t

        xt = place("xt", [P, KT, S])
        hh = place("hh", [P, KT, S], F32R)
        hl = place("hl", [P, KT, S], F32R)
        raw = place("raw", [P, 2, BLK])
        whi = place("whi", [P, 2, BLK], F32R)
        wlo = place("wlo", [P, 2, BLK], F32R)
        rstd = place("rstd", [P, S])
        sq = place("sq", [P, 2, S])
        tmp = place("tmp", [P, 2, S])
        y0 = place("y0", [P, S])
        par = place("par", [P, 81])
        lb_m = place("lb_m", [P, 16])
        lb_e = place("lb_e", [P, 2, 16])
        lb_s = place("lb_s", [P, 16])
        lb_r = place("lb_r", [P, 16])
        lb = place("lb", [P, 16])
        oml = place("oml", [P, 16])
        eps = place("eps", [P, 1])
        half_gain = place("half_gain", [P, 2, KT])
        wait_taker = place("wait_taker", [P, 2])
        ones = place("ones", [P, P])
        cst = place("cst", [P, 3 * P + 2 * S])
        ident = cst[:, 0:P]
        tri = (cst[:, P:2 * P], cst[:, 2 * P:3 * P])
        keep_state = (cst[:, 3 * P:3 * P + S], cst[:, 3 * P + S:3 * P + 2 * S])
        arena = at[0]

        ah = place("ah", [P, FT, S], F32R)
        al = place("al", [P, FT, S], F32R)
        silu = place("silu", [P, S])
        at[0] = arena
        hot_sb = place("hot_sb", [BUCKETS + 1, N_TAB * VEC])
        table = place("table", [BUCKETS + 1, N_GROUPS * N_HEADS])
        vec_sb = place("vec_sb", [N_HEADS, N_TAB * VEC])
        at[0] = arena
        ymix = place("ymix", [P, KT, S])
        after_ymix = at[0]
        v_tok = place("v_tok", [P, N_GROUPS, R, S])
        bias = place("bias", [P, 2, N_TAB, U])
        q_t = place("q_t", [P, N_GROUPS, R, U])
        k_t = place("k_t", [P, N_GROUPS, R, U])
        prob = place("prob", [P, 2, 6 * U])
        prob_t = place("prob_t", [P, 2, 6 * U])
        neg_max = place("neg_max", [P, 8])
        row_sum = place("row_sum", [P, 8])
        row_inv = place("row_inv", [P, 8])
        o_tok = place("o_tok", [P, R, N_HEADS * HD])
        ath = place("ath", [P, 4, S], F32R)
        atl = place("atl", [P, 4, S], F32R)
        sig_a = place("sig_a", [P, 4, S])
        at[0] = after_ymix
        bh = place("bh", [P, KT, S], F32R)
        bl = place("bl", [P, KT, S], F32R)
        hgrn_at = at[0]
        ih_tok = place("ih_tok", [P, TT, D])
        sig = [place(f"sig_{d}", [P, S]) for d in "fb"]
        sig_q, sig_g = tmp[:, 0, :], tmp[:, 1, :]
        q_h = place("q_h", [P, S])
        gate = place("gate", [P, S])
        key = [place(f"key_{d}", [P, S]) for d in "fb"]
        cum = [place(f"cum_{d}", [P, S]) for d in "fb"]
        e_up = [place(f"e_up_{d}", [P, S]) for d in "fb"]
        e_dn = [place(f"e_dn_{d}", [P, S]) for d in "fb"]
        e_ref = [place(f"e_ref_{d}", [P, NC_CH]) for d in "fb"]
        decay = [place(f"decay_{d}", [P, NC_CH]) for d in "fb"]
        q_in = [place(f"q_in_{d}", [P, S]) for d in "fb"]
        k_in = [place(f"k_in_{d}", [P, S]) for d in "fb"]
        q_st = [place(f"q_st_{d}", [P, S]) for d in "fb"]
        kh_tok = [place(f"kh_tok_{d}", [P, TT, P]) for d in "fb"]
        att = [place(f"att_{d}", [P, TT, P]) for d in "fb"]
        state = [place(f"state_{d}", [P, NC_CH - 1, P]) for d in "fb"]
        o_sq = place("o_sq", [P, P])
        o_ss = place("o_ss", [P, TT])
        o_rs = place("o_rs", [P, TT])
        v_h = y0[:].rearrange("p (t v) -> p t v", v=P)
        o_nrm = sq[:, 0, :].rearrange("p (t v) -> p t v", v=P)
        b_out = sq[:, 1, :]
        at[0] = hgrn_at
        yh = place("yh", [P, KT, S], F32R)
        yl = place("yl", [P, KT, S], F32R)
        sig_h = place("sig_h", [P, S])

        ps = ctx.enter_context(nc.psum_tensor("ps", [P, 8, S], F32))
        vec_dram = nc.dram_tensor("vec_dram", [N_HEADS, N_TAB, VEC], F32, kind="Internal")

        sems = {}

        def sem(name):
            if name not in sems:
                sems[name] = ctx.enter_context(nc.semaphore(name))
            return sems[name]

        def seed(engine, *names):
            for name in names:
                engine.sem_inc(sem(name), 1)

        raw_in = [sem("raw_in0"), sem("raw_in1")]
        head_done, split_done, block_done = sem("head_done"), sem("split_done"), sem("block_done")

        def load_block(sp, pair, s):
            sp.wait_ge(split_done, 2 * pair + s - 1)
            sp.dma_start(raw[:, s, :], wstream[bass.ds(2 * pair + s, 1)].rearrange("b p n -> p (b n)")
                         ).then_inc(raw_in[s], 16)

        def head(act, pair, s):
            act.wait_ge(raw_in[s], 16 * pair + 32)
            act.wait_ge(block_done, 2 * pair + s + 1)
            nc.scalar.activation(whi[:, s, :], raw[:, s, :], ACT.Copy).then_inc(head_done, 1)

        def tail(dve, pair, s):
            dve.wait_ge(head_done, 2 * pair + s + 3)
            nc.vector.tensor_tensor(wlo[:, s, :], raw[:, s, :], whi[:, s, :].bitcast(F32),
                                    ALU.subtract).then_inc(split_done, 1)

        def product(out, w, wl, m, ml, start, stop):
            nc.tensor.matmul(out, w, m, start=start, stop=False)
            nc.tensor.matmul(out, w, ml, start=False, stop=False)
            return nc.tensor.matmul(out, wl, m, start=False, stop=stop)

        def wcols(s, c0, n=P):
            return whi[:, s, c0:c0 + n], wlo[:, s, c0:c0 + n]

        def project(pe, pair, s, out, mh, ml, ready=None):
            pe.wait_ge(split_done, 2 * pair + s + 1)
            for kt in range(KT):
                if ready:
                    pe.wait_ge(ready, kt + 1)
                last = product(out, *wcols(s, kt * P), mh[:, kt, :], ml[:, kt, :], kt == 0, kt == KT - 1)
            last.then_inc(block_done, 1)

        def ffn_in_pe(pe, n):
            first = FIRST[f"ffn{n}_in"]
            with pe.Fori(0, FT) as j:
                pe.wait_ge(sem(f"silu{n}"), j + 1)
                project(pe, first + j, 0, ps[:, 0, :], hh, hl, ready=sem(f"pre{n}_ready"))
                pe.wait_ge(sem(f"glu{n}"), j + 1)
                project(pe, first + j, 1, ps[:, 1, :], hh, hl)

        def ffn_in_act(act, n):
            first = FIRST[f"ffn{n}_in"]
            nc.scalar.preload_act_table(ACT.Silu)
            seed(act, f"silu{n}")
            with act.Fori(0, FT) as j:
                head(act, first + j, 0)
                act.wait_ge(sem(f"glu{n}"), j + 1)
                nc.scalar.activation(silu[:], ps[:, 0, :], ACT.Silu).then_inc(sem(f"silu{n}"), 1)
                head(act, first + j, 1)
                act.wait_ge(sem(f"glu{n}"), j + 2)
                nc.scalar.activation(ah[:, bass.ds(j, 1), :].rearrange("p a n -> p (a n)"), tmp[:, 0, :],
                                     ACT.Copy).then_inc(sem(f"a_head{n}"), 1)

        def ffn_in_dve(dve, n):
            first = FIRST[f"ffn{n}_in"]
            seed(dve, f"glu{n}", f"a_tail{n}")
            with dve.Fori(0, FT) as j:
                tail(dve, first + j, 0)
                dve.wait_ge(sem(f"silu{n}"), j + 2)
                dve.wait_ge(block_done, 2 * (first + j) + 2)
                dve.wait_ge(sem(f"a_tail{n}"), j + 1)
                nc.vector.tensor_tensor(tmp[:, 0, :], silu[:], ps[:, 1, :], ALU.mult).then_inc(sem(f"glu{n}"), 1)
                tail(dve, first + j, 1)
                dve.wait_ge(sem(f"a_head{n}"), j + 1)
                dst = (al[:, bass.ds(j, 1), :].rearrange("p a n -> p (a n)"),
                       ah[:, bass.ds(j, 1), :].rearrange("p a n -> p (a n)").bitcast(F32))
                nc.vector.tensor_tensor(dst[0], tmp[:, 0, :], dst[1], ALU.subtract).then_inc(sem(f"a_tail{n}"), 1)

        def rows_pe(pe, stage, mh, ml, ready, seeded):
            first, pairs = FIRST[stage], dict(STAGES)[stage]

            def one(i, s, start, stop):
                pe.wait_ge(split_done, 2 * (first + i) + s + 1)
                pe.wait_ge(ready, 2 * i + s + 1 + seeded)
                m = [x[:, bass.ds(2 * i + s, 1), :].rearrange("p a n -> p (a n)") for x in (mh, ml)]
                for d in range(KT):
                    last = product(ps[:, d, :], *wcols(s, d * P), *m, start, stop)
                    if stop and d < KT - 1:
                        last.then_inc(sem(f"{stage}_bank"), 1)
                last.then_inc(block_done, 1)

            one(0, 0, True, False)
            one(0, 1, False, False)
            with pe.Fori(1, pairs - 1) as i:
                one(i, 0, False, False)
                one(i, 1, False, False)
            one(pairs - 1, 0, False, False)
            one(pairs - 1, 1, False, True)

        def split_act(act, stage, last=0):
            with act.Fori(FIRST[stage], FIRST[stage] + dict(STAGES)[stage] - last) as pair:
                head(act, pair, 0)
                head(act, pair, 1)

        def split_dve(dve, stage, last=0):
            with dve.Fori(FIRST[stage], FIRST[stage] + dict(STAGES)[stage] - last) as pair:
                tail(dve, pair, 0)
                tail(dve, pair, 1)

        def sum_pe(pe, tag):
            for d in range(KT):
                pe.wait_ge(sem(f"{tag}_sq"), d + 1)
                nc.tensor.matmul(ps[:, 0, :], ones[:], sq[:, d % 2, :], start=d == 0,
                                 stop=d == KT - 1).then_inc(sem(f"{tag}_sum"), 1)

        def rstd_act(act, tag):
            act.wait_ge(sem(f"{tag}_sum"), KT)
            nc.scalar.activation(rstd[:], ps[:, 0, :], ACT.Ln, scale=1.0 / D,
                                 bias=eps[:]).then_inc(sem(f"{tag}_ln"), 1)
            act.wait_ge(sem(f"{tag}_ln"), 1)
            nc.scalar.activation(rstd[:], rstd[:], ACT.Exp, scale=-0.5).then_inc(sem(f"{tag}_rstd"), 1)

        def post_act(act, tag, stage):
            for d in range(KT):
                if d < KT - 1:
                    act.wait_ge(sem(f"{stage}_bank"), d + 1)
                else:
                    act.wait_ge(block_done, 2 * (FIRST[stage] + dict(STAGES)[stage]))
                if d >= 2:
                    act.wait_ge(sem(f"{tag}_sum"), d - 1)
                if d == 0:
                    nc.scalar.activation(y0[:], ps[:, 0, :], ACT.Copy).then_inc(sem(f"{tag}_y0"), 1)
                nc.scalar.activation(sq[:, d % 2, :], ps[:, d, :], ACT.Square).then_inc(sem(f"{tag}_sq"), 1)
            nc.scalar.preload_act_table_set("natural_log_exp_and_others")
            rstd_act(act, tag)

        def post_dve(dve, tag, gain, out_sem=None):
            def scaled(d):
                if d == 0:
                    dve.wait_ge(sem(f"{tag}_y0"), 1)
                    dve.wait_ge(sem(f"{tag}_rstd"), 1)
                if d >= 2:
                    dve.wait_ge(sem(f"{tag}_x"), d - 1)
                nc.vector.scalar_tensor_tensor(out=tmp[:, d % 2, :], in0=y0[:] if d == 0 else ps[:, d, :],
                                               scalar=gain[:, d:d + 1], in1=rstd[:], op0=ALU.mult,
                                               op1=ALU.mult).then_inc(sem(f"{tag}_scaled"), 1)
            scaled(0)
            for d in range(KT):
                if d + 1 < KT:
                    scaled(d + 1)
                dve.wait_ge(sem(f"{tag}_scaled"), d + 1)
                nc.vector.tensor_tensor(xt[:, d, :], xt[:, d, :], tmp[:, d % 2, :],
                                        ALU.add).then_inc(sem(f"{tag}_x"), 1)

        def pre_act(act, tag, x_ready):
            for d in range(KT):
                act.wait_ge(x_ready, 16 * KT if tag == "pre1" else d + 1)
                if d >= 2:
                    act.wait_ge(sem(f"{tag}_sum"), d - 1)
                nc.scalar.activation(sq[:, d % 2, :], xt[:, d, :], ACT.Square).then_inc(sem(f"{tag}_sq"), 1)
            rstd_act(act, tag)
            for d in range(KT):
                act.wait_ge(sem(f"{tag}_norm"), d + 1)
                nc.scalar.activation(hh[:, d, :], tmp[:, d % 2, :], ACT.Copy).then_inc(sem(f"{tag}_head"), 1)

        def pre_dve(dve, tag, gain):
            def norm(d):
                if d == 0:
                    dve.wait_ge(sem(f"{tag}_rstd"), 1)
                if d >= 2:
                    dve.wait_ge(sem(f"{tag}_ready"), d - 1)
                nc.vector.scalar_tensor_tensor(out=tmp[:, d % 2, :], in0=xt[:, d, :], scalar=gain[:, d:d + 1],
                                               in1=rstd[:], op0=ALU.mult,
                                               op1=ALU.mult).then_inc(sem(f"{tag}_norm"), 1)
            norm(0)
            for d in range(KT):
                if d + 1 < KT:
                    norm(d + 1)
                dve.wait_ge(sem(f"{tag}_head"), d + 1)
                nc.vector.tensor_tensor(hl[:, d, :], tmp[:, d % 2, :], hh[:, d, :].bitcast(F32),
                                        ALU.subtract).then_inc(sem(f"{tag}_ready"), 1)

        def tokens_pe(pe, stage, turns, strided, ready):
            first = FIRST[stage]
            with pe.Fori(0, turns) as g:
                for b in range(4):
                    pair, s = first + 2 * g + b // 2, b % 2
                    pe.wait_ge(split_done, 2 * pair + s + 1)
                    for k in range(2):
                        kt = 2 * b + k
                        if ready:
                            pe.wait_ge(ready, kt + 1)
                        for t in range(TT):
                            if kt == 0:
                                pe.wait_ge(sem(f"{stage}_out{t // 2}"), 2 * g + 1)
                            m = [x[:, kt, :].rearrange("p (u r) -> p r u", r=R)[:, t, :] if strided
                                 else x[:, kt, t * P:(t + 1) * P] for x in (hh, hl)]
                            w = wcols(s, k * S, S)
                            nc.tensor.matmul(ps[:, t, :], m[0], w[0], start=kt == 0, stop=False)
                            nc.tensor.matmul(ps[:, t, :], m[1], w[0], start=False, stop=False)
                            last = nc.tensor.matmul(ps[:, t, :], m[0], w[1], start=False, stop=kt == KT - 1)
                    last.then_inc(block_done, 1)

        def tokens_dst(stage, g, t):
            if stage == "v":
                return v_tok[:, bass.ds(g, 1), t, :].rearrange("p a n -> p (a n)")
            return ih_tok[:, t, bass.ds(g * S, S)]

        def tokens_act(act, stage, turns):
            first = FIRST[stage]
            seed(act, f"{stage}_out0")
            with act.Fori(0, turns) as g:
                for b in range(4):
                    head(act, first + 2 * g + b // 2, b % 2)
                for t in range(2):
                    nc.scalar.activation(tokens_dst(stage, g, t), ps[:, t, :],
                                         ACT.Copy).then_inc(sem(f"{stage}_out0"), 1)

        def tokens_dve(dve, stage, turns):
            first = FIRST[stage]
            seed(dve, f"{stage}_out1")
            with dve.Fori(0, turns) as g:
                for b in range(4):
                    tail(dve, first + 2 * g + b // 2, b % 2)
                dve.wait_ge(block_done, 2 * (first + 2 * g) + 4)
                for t in range(2, 4):
                    nc.vector.tensor_copy(tokens_dst(stage, g, t), ps[:, t, :]).then_inc(sem(f"{stage}_out1"), 1)

        def attn_pe(pe):
            first = FIRST["qk"]
            scored, prob_done = sem("scored"), sem("prob_done")
            turned, turned_out = sem("turned"), sem("turned_out")
            summed, o_out = sem("summed"), sem("o_out")
            with pe.Fori(0, PAIRS_H) as hp:
                pe.wait_ge(o_out, 8 * hp + 1)
                for g in range(N_GROUPS):
                    pe.wait_ge(sem("q_out"), 3 * hp + g + 1)
                    project(pe, first + 3 * hp + g, 0, ps[:, 0, :], hh, hl)
                    pe.wait_ge(sem("k_out"), 3 * hp + g + 1)
                    project(pe, first + 3 * hp + g, 1, ps[:, 1, :], hh, hl)
                pe.wait_ge(sem("q_out"), 3 * hp + 4)
                pe.wait_ge(sem("k_out"), 3 * hp + 4)

                def scores(n):
                    e, r = n // R, n % R
                    rows = slice(HD * e, HD * e + HD)
                    if n >= 2:
                        pe.wait_ge(sem("biased"), 8 * hp + n - 1)
                    b = 2 + 2 * (n % 2)
                    nc.tensor.matmul(ps[:, b, :], q_t[rows, 0, r, :],
                                     k_t[rows, 0, :, :].rearrange("p r u -> p (r u)"), start=True, stop=True)
                    for g in (1, 2):
                        last = nc.tensor.matmul(ps[:, b + 1, (g - 1) * U:g * U], q_t[rows, g, r, :],
                                                k_t[rows, g, r, :], start=True, stop=True)
                    last.then_inc(scored, 1)

                scores(0)
                scores(1)
                for n in range(8):
                    pe.wait_ge(prob_done, 8 * hp + n + 1)
                    pe.wait_ge(turned_out, 8 * hp + n + 1)
                    for k in range(6):
                        last = nc.tensor.transpose(ps[:, 6 + k // 4, (k % 4) * U:(k % 4 + 1) * U],
                                                   prob[:, n % 2, k * U:(k + 1) * U], ident)
                    last.then_inc(turned, 1)
                    if n + 2 < 8:
                        scores(n + 2)
                    pe.wait_ge(turned_out, 8 * hp + n + 2)
                    if n >= 2:
                        pe.wait_ge(o_out, 8 * hp + n)
                    e, r = n // R, n % R
                    for k in range(6):
                        g, tile = (0, k) if k < R else (k - R + 1, r)
                        last = nc.tensor.matmul(ps[:, n % 2, 0:P], prob_t[:, n % 2, k * U:(k + 1) * U],
                                                v_tok[:, g, tile, bass.ds(hp * P, P)],
                                                start=k == 0, stop=k == 5)
                    last.then_inc(summed, 1)
            pe.wait_ge(o_out, 8 * PAIRS_H + 1)
            for ft in range(4):
                for r in range(R):
                    last = nc.tensor.transpose(ps[:, ft, r * U:(r + 1) * U], o_tok[:, r, ft * P:(ft + 1) * P],
                                               ident)
                last.then_inc(sem("a_turned"), 1)

        def attn_act(act):
            first = FIRST["qk"]
            nc.scalar.preload_act_table_set("natural_log_exp_and_others")
            seed(act, "q_out", "turned_out")
            with act.Fori(0, PAIRS_H) as hp:
                for g in range(N_GROUPS):
                    head(act, first + 3 * hp + g, 0)
                    nc.scalar.activation(q_t[:, g, :, :], ps[:, 0, :].rearrange("p (u r) -> p r u", r=R)[:, :, ::-1],
                                         ACT.Copy, scale=HD ** -0.5).then_inc(sem("q_out"), 1)
                    head(act, first + 3 * hp + g, 1)

                def softmax(n):
                    act.wait_ge(sem("maxed"), 8 * hp + n + 1)
                    nc.scalar.activation(prob[:, n % 2, :], prob[:, n % 2, :], ACT.Exp, bias=neg_max[:, n:n + 1],
                                         accum_out=row_sum[:, n:n + 1]).then_inc(sem("prob_done"), 1)

                def turned_copy(n):
                    act.wait_ge(sem("turned"), 8 * hp + n + 1)
                    act.wait_ge(sem("summed"), 8 * hp + n - 1) if n >= 2 else None
                    nc.scalar.activation(prob_t[:, n % 2, :],
                                         ps[:, 6:8, :].rearrange("p a n -> p (a n)")[:, 0:6 * U],
                                         ACT.Copy).then_inc(sem("turned_out"), 1)

                softmax(0)
                softmax(1)
                turned_copy(0)
                for n in range(1, 8):
                    turned_copy(n)
                    if n + 1 < 8:
                        softmax(n + 1)
            for ft in range(4):
                act.wait_ge(sem("a_turned"), ft + 1)
                nc.scalar.activation(ath[:, ft, :].rearrange("p (u r) -> p r u", r=R),
                                     ps[:, ft, :].rearrange("p (r u) -> p r u", r=R)[:, :, ::-1],
                                     ACT.Copy).then_inc(sem("ath_done"), 1)

        def attn_dve(dve):
            first = FIRST["qk"]
            seed(dve, "k_out", "o_out")
            with dve.Fori(0, PAIRS_H) as hp:
                for g in range(N_GROUPS):
                    tail(dve, first + 3 * hp + g, 0)
                    dve.wait_ge(block_done, 2 * (first + 3 * hp + g) + 2)
                    nc.vector.tensor_copy(k_t[:, g, :, :], ps[:, 1, :].rearrange("p (u r) -> p r u", r=R)
                                          ).then_inc(sem("k_out"), 1)
                    tail(dve, first + 3 * hp + g, 1)
                dve.wait_ge(sem("bias_in"), 32 * hp + 32)

                def biased(n):
                    e, r = n // R, n % R
                    dve.wait_ge(sem("scored"), 8 * hp + n + 1)
                    if n >= 2:
                        dve.wait_ge(sem("turned"), 8 * hp + n - 1)
                    b = 2 + 2 * (n % 2)
                    nc.vector.tensor_tensor(prob[:, n % 2, 0:S], ps[:, b, :],
                                            bias[:, e, R - 1 - r:2 * R - 1 - r, :].rearrange("p c u -> p (c u)"),
                                            ALU.add).then_inc(sem("biased_0"), 1)
                    nc.vector.tensor_tensor(prob[:, n % 2, S:6 * U], ps[:, b + 1, 0:2 * U],
                                            bias[:, e, N_TAB - 2:N_TAB, :].rearrange("p c u -> p (c u)"),
                                            ALU.add).then_inc(sem("biased"), 1)
                    dve.wait_ge(sem("biased_0"), 8 * hp + n + 1)
                    dve.wait_ge(sem("biased"), 8 * hp + n + 1)
                    nc.vector.tensor_reduce(neg_max[:, n:n + 1], prob[:, n % 2, :], AXIS_X, ALU.max,
                                            negate=True).then_inc(sem("maxed"), 1)

                def outputs(n):
                    e, r = n // R, n % R
                    dve.wait_ge(sem("prob_done"), 8 * hp + n + 1)
                    nc.vector.reciprocal(row_inv[:, n:n + 1], row_sum[:, n:n + 1]).then_inc(sem("inverted"), 1)
                    dve.wait_ge(sem("inverted"), 8 * hp + n + 1)
                    dve.wait_ge(sem("summed"), 8 * hp + n + 1)
                    nc.vector.tensor_scalar(o_tok[:, r, bass.ds(hp * 2 * HD + e * HD, HD)], ps[:, n % 2, e * HD:(e + 1) * HD],
                                            row_inv[:, n:n + 1], None, ALU.mult).then_inc(sem("o_out"), 1)

                biased(0)
                biased(1)
                for n in range(8):
                    if n + 2 < 8:
                        biased(n + 2)
                    outputs(n)
            for ft in range(4):
                dve.wait_ge(sem("ath_done"), ft + 1)
                nc.vector.tensor_tensor(atl[:, ft, :].rearrange("p (u r) -> p r u", r=R),
                                        ps[:, ft, :].rearrange("p (r u) -> p r u", r=R)[:, :, ::-1],
                                        ath[:, ft, :].rearrange("p (u r) -> p r u", r=R).bitcast(F32),
                                        ALU.subtract).then_inc(sem("atl_done"), 1)

        def gate_a_pe(pe):
            first = FIRST["gate_a"]
            pe.wait_ge(sem("atl_done"), 4)
            with pe.Fori(0, 2) as i:
                for m in range(4):
                    pe.wait_ge(sem("sig_a_done"), 4 * i + 1)
                    project(pe, first + 3 * i + m // 2, m % 2, ps[:, m, :], hh, hl)
                for b in range(2):
                    pair = first + 3 * i + 2
                    pe.wait_ge(split_done, 2 * pair + b + 1)
                    for d in range(2):
                        m = 2 * b + d
                        pe.wait_ge(sem("y_a"), 4 * i + 1)
                        for kt in range(4):
                            last = product(ps[:, 4 + m, :], *wcols(b, d * S + kt * P), ath[:, kt, :],
                                           atl[:, kt, :], kt == 0, kt == 3)
                    last.then_inc(block_done, 1)

        def gate_a_act(act):
            first = FIRST["gate_a"]
            nc.scalar.preload_act_table(ACT.Sigmoid)
            seed(act, "sig_a_done")
            with act.Fori(0, 2) as i:
                for m in range(4):
                    head(act, first + 3 * i + m // 2, m % 2)
                    act.wait_ge(sem("y_a"), 4 * i + 1)
                    nc.scalar.activation(sig_a[:, m, :], ps[:, m, :], ACT.Sigmoid).then_inc(sem("sig_a_done"), 1)
                for b in range(2):
                    head(act, first + 3 * i + 2, b)

        def gate_a_dve(dve):
            first = FIRST["gate_a"]
            seed(dve, "y_a")
            with dve.Fori(0, 2) as i:
                for m in range(4):
                    tail(dve, first + 3 * i + m // 2, m % 2)
                for b in range(2):
                    tail(dve, first + 3 * i + 2, b)
                    for m in (2 * b, 2 * b + 1):
                        dve.wait_ge(sem("sig_a_done"), 4 * i + m + 2)
                        nc.vector.tensor_tensor(ymix[:, bass.ds(4 * i + m, 1), :].rearrange("p a n -> p (a n)"),
                                                sig_a[:, m, :], ps[:, 4 + m, :], ALU.mult).then_inc(sem("y_a"), 1)

        def both(x):
            return x.rearrange("p (n c) -> p n c", c=C)

        REF = (C // 2, C // 2 - 1)
        END = (C - 1, 0)

        def hgrn_pe(pe):
            first = FIRST["hgrn"]
            seed(pe, "o_psum")

            def turn(h, proj, scan):
                def project_part(b, free):
                    if proj:
                        if free:
                            pe.wait_ge(sem(free[0]), free[1])
                        project(pe, first + 2 * h + b // 2, b % 2, ps[:, b % 2, :], hh, hl)

                project_part(0, ("sig_f1", h) if scan else None)
                if scan:
                    for d in range(2):
                        pe.wait_ge(sem(f"k_end{d}"), h)
                        for t in range(TT):
                            last = nc.tensor.transpose(ps[:, 2 + d, t * P:(t + 1) * P],
                                                       e_dn[d][:, t * P:(t + 1) * P], ident)
                        last.then_inc(sem(f"kh_turned{d}"), 1)
                    for d in range(2):
                        pe.wait_ge(sem(f"q_st{d}"), h)
                        if d:
                            pe.wait_ge(sem("b_done"), h)
                        for t in range(TT):
                            cols = slice(t * P, (t + 1) * P)
                            last = nc.tensor.matmul(ps[:, 4 + d, cols], k_in[d][:, cols], q_in[d][:, cols],
                                                    start=True, stop=True)
                        last.then_inc(sem(f"att_psum{d}"), 1)
                project_part(1, ("gate_done", h) if scan else None)
                if scan:
                    pe.wait_ge(sem("v_taken"), h)
                    for d in range(2):
                        pe.wait_ge(sem("kh_out1"), h)
                        for i in range(NC_CH - 1):
                            n = i if d == 0 else NC_CH - 1 - i
                            rows = slice(C * (n % 2), C * (n % 2) + C)
                            nc.tensor.matmul(ps[:, (6, 2)[d] + n % 2, (n // 2) * P:(n // 2 + 1) * P],
                                             kh_tok[d][rows, n // 2, :], v_h[rows, n // 2, :],
                                             start=True, stop=True).then_inc(sem(f"added{d}"), 1)
                project_part(2, ("q_done", h + 1))
                if scan:
                    for d in range(2):
                        pe.wait_ge(sem(f"att_out{d}"), h)
                        pe.wait_ge(sem(f"state{d}"), (NC_CH - 1) * h)
                    for t in range(TT):
                        out = ps[:, 4, t * P:(t + 1) * P]
                        nc.tensor.matmul(out, att[0][:, t, :], v_h[:, t, :], start=True, stop=False)
                        nc.tensor.matmul(out, att[1][:, t, :], v_h[:, t, :], start=False, stop=False)
                        for half in range(2):
                            n = 2 * t + half
                            part = ps[C * half:C * half + C, 4, t * P:(t + 1) * P]
                            dirs = [d for d in range(2) if n != (0, NC_CH - 1)[d]]
                            for d in dirs:
                                i = (n - 1, NC_CH - 2 - n)[d]
                                last = nc.tensor.matmul(part, q_st[d][:, n * C:(n + 1) * C], state[d][:, i, :],
                                                        start=False, stop=d == dirs[-1])
                    last.then_inc(sem("o_psum"), 1)
                project_part(3, ("sig_f0", h + 1))
                if scan:
                    pe.wait_ge(sem("o_norm"), TT * h)
                    for t in range(TT):
                        last = nc.tensor.transpose(ps[:, 5, t * P:(t + 1) * P], o_nrm[:, t, :], ident)
                    last.then_inc(sem("o_turned"), 1)

            turn(0, True, False)
            with pe.Fori(1, GH_HEADS) as h:
                turn(h, True, True)
            turn(GH_HEADS, False, True)

        def hgrn_act(act):
            first = FIRST["hgrn"]

            def turn(h, proj, scan):
                if proj:
                    head(act, first + 2 * h, 0)
                    nc.scalar.activation(sig_q, ps[:, 0, :], ACT.Sigmoid).then_inc(sem("sig_q"), 1)
                if scan:
                    for d in range(2):
                        act.wait_ge(sem(f"kh_turned{d}"), h)
                        nc.scalar.activation(kh_tok[d][:].rearrange("p t k -> p (t k)"), ps[:, 2 + d, :],
                                             ACT.Copy).then_inc(sem(f"kh_out{d}"), 1)
                if proj:
                    head(act, first + 2 * h, 1)
                    nc.scalar.activation(sig[0][:], ps[:, 1, :], ACT.Sigmoid).then_inc(sem("sig_f0"), 1)
                    head(act, first + 2 * h + 1, 0)
                    nc.scalar.activation(sig[1][:], ps[:, 0, :], ACT.Sigmoid).then_inc(sem("sig_f1"), 1)
                    for d in range(2):
                        lane = bass.ds(d * GH_HEADS + h, 1)
                        act.wait_ge(sem(f"sig_f{d}"), h + 1)
                        nc.scalar.activation(cum[d][:], sig[d][:], ACT.Ln, scale=oml[:, lane],
                                             bias=lb[:, lane]).then_inc(sem(f"logf{d}"), 1)
                if scan:
                    act.wait_ge(sem("o_psum"), h + 1)
                    for t in range(TT):
                        nc.scalar.activation(o_nrm[:, t, :], ps[:, 4, t * P:(t + 1) * P], ACT.Square,
                                             accum_out=o_ss[:, t:t + 1]).then_inc(sem("o_ss"), 1)
                    act.wait_ge(sem("o_ss"), TT * h)
                    nc.scalar.activation(o_rs[:], o_ss[:], ACT.Ln, scale=1.0 / P,
                                         bias=eps[:]).then_inc(sem("o_ln"), 1)
                    act.wait_ge(sem("o_ln"), h)
                    nc.scalar.activation(o_rs[:], o_rs[:], ACT.Exp, scale=-0.5).then_inc(sem("o_rstd"), 1)
                if proj:
                    for d in range(2):
                        act.wait_ge(sem(f"cum{d}"), h + 1)
                        nc.scalar.activation(e_ref[d][:], both(cum[d][:])[:, :, REF[d]], ACT.Exp
                                             ).then_inc(sem(f"e_ref{d}"), 1)
                        nc.scalar.activation(decay[d][:], both(cum[d][:])[:, :, END[d]], ACT.Exp
                                             ).then_inc(sem(f"decay{d}"), 1)
                        act.wait_ge(sem(f"rel{d}"), h + 1)
                        nc.scalar.activation(e_up[d][:], k_in[d][:], ACT.Exp).then_inc(sem(f"e_up{d}"), 1)
                        nc.scalar.activation(e_dn[d][:], k_in[d][:], ACT.Exp,
                                             scale=-1.0).then_inc(sem(f"e_dn{d}"), 1)
                    head(act, first + 2 * h + 1, 1)
                    nc.scalar.activation(sig_g, ps[:, 1, :], ACT.Sigmoid).then_inc(sem("sig_g"), 1)
                if scan:
                    act.wait_ge(sem("b_done"), h + 1)
                    nc.scalar.activation(bh[:, bass.ds(h - 1, 1), :].rearrange("p a n -> p (a n)"), b_out,
                                         ACT.Copy).then_inc(sem("bh_done"), 1)

            turn(0, True, False)
            with act.Fori(1, GH_HEADS) as h:
                turn(h, True, True)
            turn(GH_HEADS, False, True)

        def hgrn_dve(dve):
            first = FIRST["hgrn"]
            for d in range(2):
                nc.vector.memset(att[d][:], 0.0).then_inc(sem("att_zero"), 1)
            dve.wait_ge(sem("att_zero"), 2)
            seed(dve, "b_done")

            def products(h, d):
                dve.wait_ge(sem(f"e_up{d}"), h + 1)
                nc.vector.tensor_tensor(q_in[d][:], q_h[:], e_up[d][:], ALU.mult).then_inc(sem(f"q_in{d}"), 1)
                dve.wait_ge(sem(f"e_dn{d}"), h + 1)
                nc.vector.tensor_tensor(k_in[d][:], key[d][:], e_dn[d][:], ALU.mult).then_inc(sem(f"k_in{d}"), 1)
                dve.wait_ge(sem(f"k_in{d}"), h + 1)
                nc.vector.tensor_tensor(both(e_dn[d][:]), both(k_in[d][:]),
                                        both(e_up[d][:])[:, :, END[d]:END[d] + 1].to_broadcast([P, NC_CH, C]),
                                        ALU.mult).then_inc(sem(f"k_end{d}"), 1)
                dve.wait_ge(sem(f"q_in{d}"), h + 1)
                dve.wait_ge(sem(f"e_ref{d}"), h + 1)
                nc.vector.tensor_tensor(both(q_st[d][:]), both(q_in[d][:]),
                                        e_ref[d][:].unsqueeze(2).to_broadcast([P, NC_CH, C]),
                                        ALU.mult).then_inc(sem(f"q_st{d}"), 1)

            def turn(h, proj, scan):
                if proj:
                    tail(dve, first + 2 * h, 0)
                    dve.wait_ge(sem("sig_q"), h + 1)
                    nc.vector.tensor_tensor(q_h[:], sig_q, ps[:, 0, :], ALU.mult).then_inc(sem("q_done"), 1)
                if scan:
                    for d in range(2):
                        dve.wait_ge(sem(f"att_psum{d}"), h)
                        nc.vector.tensor_copy(wait_taker[:, d:d + 1], eps[:])
                        nc.vector.copy_predicated(att[d][:],
                                                  tri[d].unsqueeze(1).to_broadcast([P, TT, P]).bitcast(U32),
                                                  ps[:, 4 + d, :].rearrange("p (t c) -> p t c", c=P)
                                                  ).then_inc(sem(f"att_out{d}"), 1)
                if proj:
                    tail(dve, first + 2 * h, 1)
                if scan:
                    for i in range(NC_CH - 1):
                        for d in range(2):
                            n = i if d == 0 else NC_CH - 1 - i
                            if i == 0:
                                dve.wait_ge(sem(f"added{d}"), (NC_CH - 1) * h)
                            new = ps[:, (6, 2)[d] + n % 2, (n // 2) * P:(n // 2 + 1) * P]
                            if i == 0:
                                nc.vector.tensor_copy(state[d][:, 0, :], new).then_inc(sem(f"state{d}"), 1)
                            else:
                                if i == 1:
                                    dve.wait_ge(sem(f"decay{d}"), h)
                                dve.wait_ge(sem(f"state{d}"), (NC_CH - 1) * (h - 1) + i)
                                nc.vector.scalar_tensor_tensor(out=state[d][:, i, :], in0=state[d][:, i - 1, :],
                                                               scalar=decay[d][:, n:n + 1], in1=new,
                                                               op0=ALU.mult, op1=ALU.add
                                                               ).then_inc(sem(f"state{d}"), 1)
                if proj:
                    tail(dve, first + 2 * h + 1, 0)
                    for d in range(2):
                        flip = slice(None, None, -1) if d else slice(None)
                        lane = bass.ds(d * GH_HEADS + h, 1)
                        dve.wait_ge(sem(f"logf{d}"), h + 1)
                        nc.vector.tensor_tensor_scan(out=cum[d][:, flip], data0=keep_state[d][:, flip],
                                                     data1=cum[d][:, flip], initial=0.0, op0=ALU.mult,
                                                     op1=ALU.add).then_inc(sem(f"cum{d}"), 1)
                        nc.vector.tensor_scalar(sig[d][:], sig[d][:], -1.0, 1.0, ALU.mult,
                                                ALU.add).then_inc(sem(f"one_less{d}"), 1)
                        dve.wait_ge(sem(f"cum{d}"), h + 1)
                        nc.vector.tensor_tensor(both(k_in[d][:]), both(cum[d][:]),
                                                both(cum[d][:])[:, :, REF[d]:REF[d] + 1
                                                                ].to_broadcast([P, NC_CH, C]),
                                                ALU.subtract).then_inc(sem(f"rel{d}"), 1)
                        dve.wait_ge(sem(f"one_less{d}"), h + 1)
                        nc.vector.tensor_scalar(key[d][:], sig[d][:], oml[:, lane], None,
                                                ALU.mult).then_inc(sem(f"key{d}"), 1)
                if scan:
                    dve.wait_ge(sem("o_rstd"), h)
                    for t in range(TT):
                        nc.vector.tensor_scalar(o_nrm[:, t, :], ps[:, 4, t * P:(t + 1) * P], o_rs[:, t:t + 1],
                                                None, ALU.mult).then_inc(sem("o_norm"), 1)
                if proj:
                    dve.wait_ge(sem("q_done"), h + 1)
                    dve.wait_ge(sem("key1"), h + 1)
                    products(h, 0)
                    tail(dve, first + 2 * h + 1, 1)
                    products(h, 1)
                if scan:
                    dve.wait_ge(sem("o_turned"), h)
                    nc.vector.tensor_tensor(b_out, gate[:], ps[:, 5, :], ALU.mult).then_inc(sem("b_done"), 1)
                if proj:
                    if scan:
                        dve.wait_ge(sem("b_done"), h + 1)
                    dve.wait_ge(sem("sig_g"), h + 1)
                    nc.vector.scalar_tensor_tensor(out=gate[:], in0=ps[:, 1, :], scalar=par[:, 48:49], in1=sig_g,
                                                   op0=ALU.mult, op1=ALU.mult).then_inc(sem("gate_done"), 1)
                if scan:
                    dve.wait_ge(sem("bh_done"), h)
                    one = bass.ds(h - 1, 1)
                    nc.vector.tensor_tensor(bl[:, one, :].rearrange("p a n -> p (a n)"), b_out,
                                            bh[:, one, :].rearrange("p a n -> p (a n)").bitcast(F32),
                                            ALU.subtract).then_inc(sem("bl_done"), 1)

            turn(0, True, False)
            with dve.Fori(1, GH_HEADS) as h:
                turn(h, True, True)
            turn(GH_HEADS, False, True)

        def gate_h_pe(pe):
            first = FIRST["gate_h"]
            pe.wait_ge(sem("bl_done"), GH_HEADS)
            with pe.Fori(0, KT) as d:
                pe.wait_ge(sem("sig_h_done"), d + 1)
                project(pe, first + d, 0, ps[:, 0, :], hh, hl)
                pe.wait_ge(sem("y_h"), d + 1)
                project(pe, first + d, 1, ps[:, 1, :], bh, bl)

        def gate_h_act(act):
            first = FIRST["gate_h"]
            seed(act, "sig_h_done")
            with act.Fori(0, KT) as d:
                one = bass.ds(d, 1)
                head(act, first + d, 0)
                act.wait_ge(sem("y_h"), d + 1)
                nc.scalar.activation(sig_h[:], ps[:, 0, :], ACT.Sigmoid).then_inc(sem("sig_h_done"), 1)
                head(act, first + d, 1)
                act.wait_ge(sem("y_sum"), d + 2)
                nc.scalar.activation(yh[:, one, :].rearrange("p a n -> p (a n)"),
                                     ymix[:, one, :].rearrange("p a n -> p (a n)"),
                                     ACT.Copy).then_inc(sem("yh_done"), 1)

        def gate_h_dve(dve):
            first = FIRST["gate_h"]
            seed(dve, "y_h", "y_sum")
            with dve.Fori(0, KT) as d:
                one = bass.ds(d, 1)
                y = ymix[:, one, :].rearrange("p a n -> p (a n)")
                tail(dve, first + d, 0)
                dve.wait_ge(sem("sig_h_done"), d + 2)
                dve.wait_ge(block_done, 2 * (first + d) + 2)
                dve.wait_ge(sem("y_sum"), d + 1)
                nc.vector.tensor_tensor(tmp[:, 0, :], sig_h[:], ps[:, 1, :], ALU.mult).then_inc(sem("y_h"), 1)
                dve.wait_ge(sem("y_h"), d + 2)
                nc.vector.tensor_tensor(y, y, tmp[:, 0, :], ALU.add).then_inc(sem("y_sum"), 1)
                tail(dve, first + d, 1)
                dve.wait_ge(sem("yh_done"), d + 1)
                nc.vector.tensor_tensor(yl[:, one, :].rearrange("p a n -> p (a n)"), y,
                                        yh[:, one, :].rearrange("p a n -> p (a n)").bitcast(F32),
                                        ALU.subtract).then_inc(sem("yl_done"), 1)

        block = ctx.enter_context(nc.Block())

        @block.sync
        def _(sp):
            for d in range(KT):
                sp.dma_start(xt[:, d, :], x_t[d * P:(d + 1) * P, :]).then_inc(sem("x_in"), 16)
            for s in range(2):
                sp.dma_start(raw[:, s, :], wstream[s]).then_inc(raw_in[s], 16)
            with sp.Fori(1, N_PAIRS) as pair:
                load_block(sp, pair, 0)
                load_block(sp, pair, 1)
            for d in range(KT):
                sp.wait_ge(sem("post3_x"), d + 1)
                sp.dma_start(out_t[d * P:(d + 1) * P, :], xt[:, d, :]).then_inc(sem("stored"), 16)
            sp.wait_ge(sem("stored"), 16 * KT)

        @block.gpsimd
        def _(pool):
            pool.dma_start(par[:], params).then_inc(sem("par_in"), 16)
            pool.dma_start(cst[:], consts).then_inc(sem("cst_in"), 16)
            pool.dma_start(table[0:BUCKETS, :], rel_bias).then_inc(sem("table_in"), 16)
            pool.dma_start(hot_sb[:], onehot).then_inc(sem("hot_in"), 16)
            pool.wait_ge(sem("vec_out"), 1)
            pool.dma_start(vec_dram.ap().rearrange("h c m -> h (c m)"), vec_sb[:]).then_inc(sem("vec_stored"), 16)
            pool.wait_ge(sem("vec_stored"), 16)
            for hp in range(PAIRS_H):
                if hp == 0:
                    pool.wait_ge(sem("post1_x"), KT)
                else:
                    pool.wait_ge(sem("biased"), 8 * hp)
                for e in range(2):
                    src = bass.AP(tensor=vec_dram, offset=(2 * hp + e) * N_TAB * VEC,
                                  ap=[[1, U], [VEC, N_TAB], [1, U]])
                    pool.dma_start(bias[:, e, :, :], src).then_inc(sem("bias_in"), 16)
            with pool.Fori(0, GH_HEADS) as h:
                pool.wait_ge(sem("ih_out0"), 5)
                pool.wait_ge(sem("ih_out1"), 5)
                pool.wait_ge(sem("o_psum"), h + 1)
                nc.gpsimd.tensor_copy(v_h, ih_tok[:, :, bass.ds(h * P, P)]).then_inc(sem("v_taken"), 1)

        @block.tensor
        def _(pe):
            pe.wait_ge(sem("hot_in"), 16)
            pe.wait_ge(sem("table_in"), 16)
            pe.wait_ge(sem("neg_row"), 1)
            n0 = (2 * R - 1) * VEC
            for c0 in range(0, N_TAB * VEC, S):
                for lo in range(c0, min(c0 + S, N_TAB * VEC), VEC):
                    g = 0 if lo < n0 else (lo - n0) // VEC + 1
                    last = nc.tensor.matmul(ps[0:N_HEADS, c0 // S, lo - c0:lo - c0 + VEC],
                                            table[:, g * N_HEADS:(g + 1) * N_HEADS], hot_sb[:, lo:lo + VEC],
                                            start=True, stop=True)
            last.then_inc(sem("vec_psum"), 1)
            pe.wait_ge(sem("vec_out"), 1)
            pe.wait_ge(sem("ones_set"), 1)
            sum_pe(pe, "pre1")
            pe.wait_ge(sem("pre1_ln"), 1)
            pe.wait_ge(sem("vec_stored"), 16)
            ffn_in_pe(pe, 1)
            pe.wait_ge(sem("glu1"), FT + 1)
            rows_pe(pe, "ffn1_out", ah, al, sem("a_tail1"), 1)
            pe.wait_ge(sem("post1_y0"), 1)
            sum_pe(pe, "post1")
            pe.wait_ge(sem("post1_ln"), 1)
            sum_pe(pe, "pre2")
            pe.wait_ge(sem("post1_scaled"), KT)
            tokens_pe(pe, "v", N_GROUPS, True, sem("pre2_ready"))
            pe.wait_ge(sem("v_out0"), 2 * N_GROUPS + 1)
            pe.wait_ge(sem("v_out1"), 2 * N_GROUPS + 1)
            pe.wait_ge(sem("cst_in"), 16)
            attn_pe(pe)
            gate_a_pe(pe)
            pe.wait_ge(sem("y_a"), 9)
            tokens_pe(pe, "ih", 2, False, None)
            pe.wait_ge(sem("ih_out0"), 5)
            pe.wait_ge(sem("ih_out1"), 5)
            hgrn_pe(pe)
            gate_h_pe(pe)
            pe.wait_ge(sem("y_h"), KT + 1)
            rows_pe(pe, "w_out", yh, yl, sem("yl_done"), 0)
            pe.wait_ge(sem("post2_y0"), 1)
            sum_pe(pe, "post2")
            pe.wait_ge(sem("post2_ln"), 1)
            sum_pe(pe, "pre3")
            pe.wait_ge(sem("pre3_ln"), 1)
            pe.wait_ge(sem("post2_scaled"), KT)
            ffn_in_pe(pe, 3)
            pe.wait_ge(sem("glu3"), FT + 1)
            rows_pe(pe, "ffn3_out", ah, al, sem("a_tail3"), 1)
            pe.wait_ge(sem("post3_y0"), 1)
            sum_pe(pe, "post3")

        @block.scalar
        def _(act):
            nc.scalar.preload_act_table_set("natural_log_exp_and_others")
            act.wait_ge(sem("vec_psum"), 1)
            nc.scalar.activation(vec_sb[:], ps[0:N_HEADS, 0:5, :].rearrange("p a n -> p (a n)")[:, 0:N_TAB * VEC],
                                 ACT.Copy).then_inc(sem("vec_out"), 1)
            act.wait_ge(sem("eps_set"), 1)
            pre_act(act, "pre1", sem("x_in"))
            act.wait_ge(sem("lb_less"), 2)
            nc.scalar.activation(lb_e[:], lb_e[:], ACT.Exp).then_inc(sem("lb_exp"), 1)
            for s in range(2):
                act.wait_ge(raw_in[s], 16)
                nc.scalar.activation(whi[:, s, :], raw[:, s, :], ACT.Copy).then_inc(head_done, 1)
            ffn_in_act(act, 1)
            split_act(act, "ffn1_out")
            post_act(act, "post1", "ffn1_out")
            pre_act(act, "pre2", sem("post1_x"))
            tokens_act(act, "v", N_GROUPS)
            attn_act(act)
            gate_a_act(act)
            tokens_act(act, "ih", 2)
            hgrn_act(act)
            gate_h_act(act)
            split_act(act, "w_out")
            post_act(act, "post2", "w_out")
            pre_act(act, "pre3", sem("post2_x"))
            ffn_in_act(act, 3)
            split_act(act, "ffn3_out", last=1)
            post_act(act, "post3", "ffn3_out")

        @block.vector
        def _(dve):
            dve.memset(table[BUCKETS:BUCKETS + 1, :], NEG_INF).then_inc(sem("neg_row"), 1)
            dve.memset(ones[:], 1.0).then_inc(sem("ones_set"), 1)
            dve.memset(eps[:], EPS).then_inc(sem("eps_set"), 1)
            dve.wait_ge(sem("par_in"), 16)
            for i, c0 in enumerate((8, 40)):
                nc.vector.tensor_scalar(half_gain[:, i, :], par[:, c0:c0 + KT], 0.5, None, ALU.mult
                                        ).then_inc(sem("half_set"), 1)
            z = par[:, 49:81].rearrange("p (d l h) -> p l d h", d=2, l=2)
            two = "p (d h) -> p d h"
            nc.vector.tensor_tensor(lb_m[:].rearrange(two, d=2), z[:, 0], z[:, 1], ALU.max).then_inc(sem("lb_max"), 1)
            dve.wait_ge(sem("lb_max"), 1)
            for l in range(2):
                nc.vector.tensor_tensor(lb_e[:, l, :].rearrange(two, d=2), z[:, l], lb_m[:].rearrange(two, d=2),
                                        ALU.subtract).then_inc(sem("lb_less"), 1)
            dve.wait_ge(sem("half_set"), 2)
            pre_dve(dve, "pre1", par[:, 0:KT])
            dve.wait_ge(sem("lb_exp"), 1)
            nc.vector.tensor_tensor(lb_s[:], lb_e[:, 0, :], lb_e[:, 1, :], ALU.add).then_inc(sem("lb_step"), 1)
            dve.wait_ge(sem("lb_step"), 1)
            nc.vector.reciprocal(lb_r[:], lb_s[:]).then_inc(sem("lb_step"), 1)
            dve.wait_ge(sem("lb_step"), 2)
            nc.vector.tensor_tensor(lb[:], lb_e[:, 0, :], lb_r[:], ALU.mult).then_inc(sem("lb_step"), 1)
            dve.wait_ge(sem("lb_step"), 3)
            nc.vector.tensor_scalar(oml[:], lb[:], -1.0, 1.0, ALU.mult, ALU.add).then_inc(sem("lb_step"), 1)
            for s in range(2):
                dve.wait_ge(head_done, s + 1)
                nc.vector.tensor_tensor(wlo[:, s, :], raw[:, s, :], whi[:, s, :].bitcast(F32),
                                        ALU.subtract).then_inc(split_done, 1)
            dve.wait_ge(sem("pre1_ready"), KT)
            ffn_in_dve(dve, 1)
            split_dve(dve, "ffn1_out")
            dve.wait_ge(sem("a_tail1"), FT + 1)
            post_dve(dve, "post1", half_gain[:, 0, :])
            dve.wait_ge(sem("post1_x"), KT)
            pre_dve(dve, "pre2", par[:, 16:16 + KT])
            tokens_dve(dve, "v", N_GROUPS)
            attn_dve(dve)
            gate_a_dve(dve)
            tokens_dve(dve, "ih", 2)
            hgrn_dve(dve)
            gate_h_dve(dve)
            split_dve(dve, "w_out")
            dve.wait_ge(sem("y_sum"), KT + 1)
            post_dve(dve, "post2", par[:, 24:24 + KT])
            dve.wait_ge(sem("post2_x"), KT)
            pre_dve(dve, "pre3", par[:, 32:32 + KT])
            dve.wait_ge(sem("pre3_ready"), KT)
            ffn_in_dve(dve, 3)
            split_dve(dve, "ffn3_out", last=1)
            dve.wait_ge(sem("a_tail3"), FT + 1)
            post_dve(dve, "post3", half_gain[:, 1, :])


def stream(w):
    out = np.empty((2 * N_PAIRS, P, BLK), np.float32)
    n = [0]

    def put(block):
        out[n[0]] = block.reshape(P, BLK)
        n[0] += 1

    def columns(a, c0):
        put(a[:, c0:c0 + P].reshape(KT, P, P).transpose(1, 0, 2))

    def wide(a, c0):
        for b in range(4):
            put(a[2 * b * P:(2 * b + 2) * P, c0:c0 + S].reshape(2, P, S).transpose(1, 0, 2))

    def rows(a):
        for f in range(a.shape[0] // P):
            put(a[f * P:(f + 1) * P])

    def ffn(win, wout):
        for j in range(FT):
            columns(win, j * P)
            columns(win, FF + j * P)
        rows(wout)

    w_in = w["w_in"][0]
    aw = N_GROUPS * N_HEADS * HD
    qa, ka, va = 0, aw, 2 * aw
    qh, fzf, fzb, ih, gh, gate_a, gate_h = (3 * aw + i * D for i in range(7))
    ffn(w["w_ffn1_in"][0], w["w_ffn1_out"][0])
    for g in range(N_GROUPS):
        wide(w_in, va + g * N_HEADS * HD)
    for hp in range(PAIRS_H):
        for g in range(N_GROUPS):
            columns(w_in, qa + g * N_HEADS * HD + hp * P)
            columns(w_in, ka + g * N_HEADS * HD + hp * P)
    pa = w["w_proj_attn"][0].reshape(4, P, D)
    for i in range(2):
        for m in range(4):
            columns(w_in, gate_a + (4 * i + m) * P)
        for b in range(2):
            d0 = (4 * i + 2 * b) * P
            put(pa[:, :, d0:d0 + 2 * P].reshape(4, P, 2, P).transpose(1, 2, 0, 3))
    for g in range(2):
        wide(w_in, ih + g * S)
    for h in range(GH_HEADS):
        for c0 in (qh, fzf, fzb, gh):
            columns(w_in, c0 + h * P)
    for d in range(KT):
        columns(w_in, gate_h + d * P)
        columns(w["w_proj_hgrn"][0], d * P)
    rows(w["w_out"][0])
    ffn(w["w_ffn2_in"][0], w["w_ffn2_out"][0])
    return out


def kernel(**inputs):
    import concourse.bacc as bacc
    from concourse.bass_utils import run_bass_kernel_spmd

    w = {k: np.asarray(v) for k, v in inputs.items()}
    by_tile = [w[k][0].reshape(KT, P).T for k in ("ffn1_pre_norm", "ffn1_post_norm", "mix_pre_norm",
                                                  "mix_post_norm", "ffn2_pre_norm", "ffn2_post_norm")]
    lb = w["hgrn_lb"].reshape(2, 2, GH_HEADS, P).transpose(3, 0, 1, 2).reshape(P, 32)
    arrays = {
        "wstream": stream(w),
        "x_t": np.ascontiguousarray(w["x"][0].T),
        "params": np.ascontiguousarray(np.concatenate([*by_tile, w["hgrn_norm"][0][:, None], lb], axis=1)),
        "rel_bias": np.ascontiguousarray(w["rel_bias"]),
        "onehot": bias_buckets(),
        "consts": constants(),
    }
    nc = bacc.Bacc("TRN2", target_bir_lowering=False, num_devices=1)
    args = [nc.dram_tensor(f"in_{k}", a.shape, mybir.dt.from_np(a.dtype), kind="ExternalInput").ap()
            for k, a in arrays.items()]
    args.append(nc.dram_tensor("out_t", (D, S), F32, kind="ExternalOutput").ap())
    build(nc, *args)
    r = run_bass_kernel_spmd(nc, [{f"in_{k}": a for k, a in arrays.items()}], core_ids=[0])
    return np.ascontiguousarray(r.results[0]["out_t"].T)[None]
```

```python
import math
from contextlib import ExitStack

import numpy as np

import concourse.bass as bass
from concourse import mybir

ALU = mybir.AluOpType
ACT = mybir.ActivationFunctionType
AXIS_X = mybir.AxisListType.X
F32 = mybir.dt.float32
F32R = mybir.dt.float32r
U32 = mybir.dt.uint32

P = 128
D = 1024
KT = D // P
X_PARTS = KT // 2
S = 512
FF = 2816
FT = FF // P
BLK = 1024
N_GROUPS, N_HEADS, HD = 3, 8, 64
PAIRS_H = N_HEADS // 2
R = 4
U = S // R
HALF = 64
DILATIONS = (1, 4, 16)
BUCKETS = 32
NEG_INF = -1e30
N_TAB = 2 * R - 1 + 2
VEC = 2 * U
GH_HEADS = 8
C = 64
NC_CH = S // C
TT = S // P
EPS = 1e-6

STAGES = (("ffn1_in", FT), ("ffn1_out", FT // 2), ("v", 2 * N_GROUPS), ("qk", N_GROUPS * PAIRS_H),
          ("gate_a", 6), ("ih", 4), ("hgrn", 2 * GH_HEADS + 2), ("gate_h", KT - 2), ("w_out", KT // 2),
          ("ffn3_in", FT), ("ffn3_out", FT // 2))
FIRST = {}
_n = 0
for _name, _count in STAGES:
    FIRST[_name] = _n
    _n += _count
N_PAIRS = _n


def bias_buckets():
    hot = np.zeros((BUCKETS + 1, N_TAB, VEC), np.float32)
    nb = BUCKETS // 2
    exact = nb // 2
    for c in range(N_TAB):
        for m in range(VEC):
            du = m - (U - 1)
            if c < 2 * R - 1:
                delta, dil, ok = R * du + c - (R - 1), DILATIONS[0], True
            elif c == 2 * R - 1:
                delta, dil, ok = du, DILATIONS[1], True
            else:
                delta, dil, ok = du // R, DILATIONS[2], du % R == 0
            if not ok or abs(delta) > HALF:
                hot[BUCKETS, c, m] = 1.0
                continue
            rel = delta * dil
            n = abs(rel)
            large = exact + int(np.float32(np.log(np.float32(max(n, 1)) / np.float32(exact)))
                                / np.float32(math.log(1024 / exact)) * np.float32(nb - exact))
            hot[(nb if rel > 0 else 0) + (n if n < exact else min(large, nb - 1)), c, m] = 1.0
    return hot.reshape(BUCKETS + 1, N_TAB * VEC)


def constants():
    s, c = np.arange(P)[:, None], np.arange(P)[None, :]
    same = s // C == c // C
    t = np.arange(S)[None, :] * np.ones((P, 1), int)
    parts = [s == c, same & (s <= c), same & (s >= c), t % C != 0, t % C != C - 1]
    return np.concatenate([x.astype(np.float32) for x in parts], axis=1)


def build(nc, wstream, x_t, params, rel_bias, onehot, consts, out_t):
    with ExitStack() as ctx:
        at = [(nc.sbuf_base + 63) // 64 * 64]

        def place(name, shape, dtype=F32):
            size = 4 * int(np.prod(shape[1:]))
            t = nc.alloc_sbuf_tensor_at(name, shape, dtype, offset=at[0])
            at[0] += (size + 31) // 32 * 32
            assert at[0] <= nc.sbuf_usable_end, (name, at[0])
            return t

        xt = place("xt", [P, KT, S])
        hh = place("hh", [P, KT, S], F32R)
        hl = place("hl", [P, KT, S], F32R)
        raw = place("raw", [P, 2, BLK])
        whi = place("whi", [P, 2, BLK], F32R)
        wlo = place("wlo", [P, 2, BLK], F32R)
        rstd = place("rstd", [P, S])
        sq = place("sq", [P, 2, S])
        tmp = place("tmp", [P, 2, S])
        y0 = place("y0", [P, S])
        par = place("par", [P, 81])
        lb_m = place("lb_m", [P, 16])
        lb_e = place("lb_e", [P, 2, 16])
        lb_s = place("lb_s", [P, 16])
        lb_r = place("lb_r", [P, 16])
        lb = place("lb", [P, 16])
        oml = place("oml", [P, 16])
        eps = place("eps", [P, 1])
        half_gain = place("half_gain", [P, 2, KT])
        wait_taker = place("wait_taker", [P, 2])
        ones = place("ones", [P, P])
        cst = place("cst", [P, 3 * P + 2 * S])
        ident = cst[:, 0:P]
        tri = (cst[:, P:2 * P], cst[:, 2 * P:3 * P])
        keep_state = (cst[:, 3 * P:3 * P + S], cst[:, 3 * P + S:3 * P + 2 * S])
        arena = at[0]

        ah = place("ah", [P, FT, S], F32R)
        al = place("al", [P, FT, S], F32R)
        silu = place("silu", [P, S])
        hot_sb = place("hot_sb", [BUCKETS + 1, N_TAB * VEC])
        table = place("table", [BUCKETS + 1, N_GROUPS * N_HEADS])
        vec_sb = place("vec_sb", [N_HEADS, N_TAB * VEC])
        at[0] = arena
        ymix = place("ymix", [P, KT, S])
        after_ymix = at[0]
        v_tok = place("v_tok", [P, N_GROUPS, R, S])
        bias = place("bias", [P, 2, N_TAB, U])
        q_t = place("q_t", [P, N_GROUPS, R, U])
        k_t = place("k_t", [P, N_GROUPS, R, U])
        prob = place("prob", [P, 2, 6 * U])
        prob_t = place("prob_t", [P, 2, 6 * U])
        neg_max = place("neg_max", [P, 8])
        row_sum = place("row_sum", [P, 8])
        row_inv = place("row_inv", [P, 8])
        o_tok = place("o_tok", [P, R, N_HEADS * HD])
        ath = place("ath", [P, 4, S], F32R)
        atl = place("atl", [P, 4, S], F32R)
        sig_a = place("sig_a", [P, 4, S])
        at[0] = after_ymix
        bh = place("bh", [P, KT, S], F32R)
        bl = place("bl", [P, KT, S], F32R)
        hgrn_at = at[0]
        ih_tok = place("ih_tok", [P, TT, D])
        sig_q, sig_g = tmp[:, 0, :], tmp[:, 1, :]
        q_h = place("q_h", [P, S])
        gate = place("gate", [P, S])
        key = [place(f"key_{d}", [P, S]) for d in "fb"]
        cum = [place(f"cum_{d}", [P, S]) for d in "fb"]
        e_up = [place(f"e_up_{d}", [P, S]) for d in "fb"]
        sig = [place(f"sig_{d}", [P, S]) for d in "fb"]
        e_dn = [place(f"e_dn_{d}", [P, S]) for d in "fb"]
        e_ref = [place(f"e_ref_{d}", [P, NC_CH]) for d in "fb"]
        decay = [place(f"decay_{d}", [P, NC_CH]) for d in "fb"]
        q_in = [place(f"q_in_{d}", [P, S]) for d in "fb"]
        k_in = [place(f"k_in_{d}", [P, S]) for d in "fb"]
        q_st = [place(f"q_st_{d}", [P, S]) for d in "fb"]
        kh_tok = [place(f"kh_tok_{d}", [P, TT, P]) for d in "fb"]
        att = [place(f"att_{d}", [P, TT, P]) for d in "fb"]
        state = [place(f"state_{d}", [P, NC_CH - 1, P]) for d in "fb"]
        o_sq = place("o_sq", [P, P])
        o_ss = place("o_ss", [P, TT])
        o_rs = place("o_rs", [P, TT])
        v_h = y0[:].rearrange("p (t v) -> p t v", v=P)
        o_nrm = sq[:, 0, :].rearrange("p (t v) -> p t v", v=P)
        b_out = sq[:, 1, :]
        at[0] = hgrn_at
        yh = place("yh", [P, KT, S], F32R)
        yl = place("yl", [P, KT, S], F32R)
        at[0] += 2 * 4 * S
        sig_h = place("sig_h", [P, S])
        first_gates = [sig_q, sig[0][:], sig[1][:], sig_g]

        ps = ctx.enter_context(nc.psum_tensor("ps", [P, 8, S], F32))
        vec_dram = nc.dram_tensor("vec_dram", [N_HEADS, N_TAB, VEC], F32, kind="Internal")

        sems = {}

        def sem(name):
            if name not in sems:
                sems[name] = ctx.enter_context(nc.semaphore(name))
            return sems[name]

        def seed(engine, *names):
            for name in names:
                engine.sem_inc(sem(name), 1)

        raw_in = [sem("raw_in0"), sem("raw_in1")]
        head_done, split_done, block_done = sem("head_done"), sem("split_done"), sem("block_done")

        def load_block(sp, pair, s):
            sp.wait_ge(split_done, 2 * pair + s - 1)
            sp.dma_start(raw[:, s, :], wstream[bass.ds(2 * pair + s, 1)].rearrange("b p n -> p (b n)")
                         ).then_inc(raw_in[s], 16)

        def head(act, pair, s):
            act.wait_ge(raw_in[s], 16 * pair + 32)
            act.wait_ge(block_done, 2 * pair + s + 1)
            nc.scalar.activation(whi[:, s, :], raw[:, s, :], ACT.Copy).then_inc(head_done, 1)

        def tail(dve, pair, s):
            dve.wait_ge(head_done, 2 * pair + s + 3)
            nc.vector.tensor_tensor(wlo[:, s, :], raw[:, s, :], whi[:, s, :].bitcast(F32),
                                    ALU.subtract).then_inc(split_done, 1)

        def product(out, w, wl, m, ml, start, stop):
            nc.tensor.matmul(out, w, m, start=start, stop=False)
            nc.tensor.matmul(out, w, ml, start=False, stop=False)
            return nc.tensor.matmul(out, wl, m, start=False, stop=stop)

        def wcols(s, c0, n=P):
            return whi[:, s, c0:c0 + n], wlo[:, s, c0:c0 + n]

        def project(pe, pair, s, out, mh, ml, ready=None):
            pe.wait_ge(split_done, 2 * pair + s + 1)
            for kt in range(KT):
                if ready:
                    pe.wait_ge(ready, kt + 1)
                last = product(out, *wcols(s, kt * P), mh[:, kt, :], ml[:, kt, :], kt == 0, kt == KT - 1)
            last.then_inc(block_done, 1)

        def bias_vectors_pe(pe):
            pe.wait_ge(sem("hot_in"), 16)
            pe.wait_ge(sem("table_in"), 16)
            pe.wait_ge(sem("filled"), 1)
            n0 = (2 * R - 1) * VEC
            for c0 in range(0, N_TAB * VEC, S):
                for lo in range(c0, min(c0 + S, N_TAB * VEC), VEC):
                    g = 0 if lo < n0 else (lo - n0) // VEC + 1
                    last = nc.tensor.matmul(ps[0:N_HEADS, 2 + c0 // S, lo - c0:lo - c0 + VEC],
                                            table[:, g * N_HEADS:(g + 1) * N_HEADS], hot_sb[:, lo:lo + VEC],
                                            start=True, stop=True)
            last.then_inc(sem("vec_psum"), 1)

        def ffn_in_pe(pe, n):
            first = FIRST[f"ffn{n}_in"]
            for kt in range(KT):
                pe.wait_ge(sem(f"pre{n}_ready"), kt + 1)
                for s in range(2):
                    if kt == 0:
                        pe.wait_ge(split_done, 2 * first + s + 1)
                    last = product(ps[:, s, :], *wcols(s, kt * P), hh[:, kt, :], hl[:, kt, :],
                                   kt == 0, kt == KT - 1)
                    if kt == KT - 1:
                        last.then_inc(block_done, 1)
            if n == 1:
                bias_vectors_pe(pe)
            with pe.Fori(1, FT) as j:
                pe.wait_ge(sem(f"silu{n}"), j + 1)
                project(pe, first + j, 0, ps[:, 0, :], hh, hl)
                pe.wait_ge(sem(f"glu{n}"), j + 1)
                project(pe, first + j, 1, ps[:, 1, :], hh, hl)

        def ffn_in_act(act, n):
            first = FIRST[f"ffn{n}_in"]
            nc.scalar.preload_act_table(ACT.Silu)

            def turn(j):
                head(act, first + j, 0)
                act.wait_ge(sem(f"glu{n}"), j + 1)
                nc.scalar.activation(silu[:], ps[:, 0, :], ACT.Silu).then_inc(sem(f"silu{n}"), 1)
                head(act, first + j, 1)
                act.wait_ge(sem(f"glu{n}"), j + 2)
                nc.scalar.activation(ah[:, bass.ds(j, 1), :].rearrange("p a n -> p (a n)"), tmp[:, 0, :],
                                     ACT.Copy).then_inc(sem(f"a_head{n}"), 1)

            if n == 1:
                turn(0)
                act.wait_ge(sem("vec_psum"), 1)
                nc.scalar.activation(vec_sb[:],
                                     ps[0:N_HEADS, 2:7, :].rearrange("p a n -> p (a n)")[:, 0:N_TAB * VEC],
                                     ACT.Copy).then_inc(sem("vec_out"), 1)
            with act.Fori(1 if n == 1 else 0, FT) as j:
                turn(j)

        def ffn_in_dve(dve, n):
            first = FIRST[f"ffn{n}_in"]
            with dve.Fori(0, FT) as j:
                tail(dve, first + j, 0)
                dve.wait_ge(sem(f"silu{n}"), j + 2)
                dve.wait_ge(block_done, 2 * (first + j) + 2)
                dve.wait_ge(sem(f"a_tail{n}"), j + 1)
                nc.vector.tensor_tensor(tmp[:, 0, :], silu[:], ps[:, 1, :], ALU.mult).then_inc(sem(f"glu{n}"), 1)
                tail(dve, first + j, 1)
                dve.wait_ge(sem(f"a_head{n}"), j + 1)
                dst = (al[:, bass.ds(j, 1), :].rearrange("p a n -> p (a n)"),
                       ah[:, bass.ds(j, 1), :].rearrange("p a n -> p (a n)").bitcast(F32))
                nc.vector.tensor_tensor(dst[0], tmp[:, 0, :], dst[1], ALU.subtract).then_inc(sem(f"a_tail{n}"), 1)

        def rows_pe(pe, stage, mh, ml, ready, seeded):
            first, pairs = FIRST[stage], dict(STAGES)[stage]

            def one(i, s, start, stop):
                pe.wait_ge(split_done, 2 * (first + i) + s + 1)
                pe.wait_ge(ready, 2 * i + s + 1 + seeded)
                m = [x[:, bass.ds(2 * i + s, 1), :].rearrange("p a n -> p (a n)") for x in (mh, ml)]
                for d in range(KT):
                    last = product(ps[:, d, :], *wcols(s, d * P), *m, start, stop)
                    if stop and d < KT - 1:
                        last.then_inc(sem(f"{stage}_bank"), 1)
                last.then_inc(block_done, 1)

            one(0, 0, True, False)
            one(0, 1, False, False)
            with pe.Fori(1, pairs - 1) as i:
                one(i, 0, False, False)
                one(i, 1, False, False)
            one(pairs - 1, 0, False, False)
            one(pairs - 1, 1, False, True)

        def split_act(act, stage, last=0):
            with act.Fori(FIRST[stage], FIRST[stage] + dict(STAGES)[stage] - last) as pair:
                head(act, pair, 0)
                head(act, pair, 1)

        def split_dve(dve, stage, last=0):
            with dve.Fori(FIRST[stage], FIRST[stage] + dict(STAGES)[stage] - last) as pair:
                tail(dve, pair, 0)
                tail(dve, pair, 1)

        def sum_acc_pe(pe, tag):
            pe.wait_ge(sem(f"{tag}_acc"), KT - 1)
            nc.tensor.matmul(ps[:, 0, :], ones[:], rstd[:], start=True, stop=True).then_inc(sem(f"{tag}_sum"), 1)

        def acc_dve(dve, tag):
            dve.wait_ge(sem(f"{tag}_sq"), 2)
            nc.vector.tensor_tensor(rstd[:], sq[:, 0, :], sq[:, 1, :], ALU.add).then_inc(sem(f"{tag}_acc"), 1)
            for d in range(2, KT):
                dve.wait_ge(sem(f"{tag}_sq"), d + 1)
                dve.wait_ge(sem(f"{tag}_acc"), d - 1)
                nc.vector.tensor_tensor(rstd[:], rstd[:], sq[:, d % 2, :], ALU.add).then_inc(sem(f"{tag}_acc"), 1)

        def sum_pe(pe, tag):
            for d in range(KT):
                pe.wait_ge(sem(f"{tag}_sq"), d + 1)
                nc.tensor.matmul(ps[:, 0, :], ones[:], sq[:, d % 2, :], start=d == 0,
                                 stop=d == KT - 1).then_inc(sem(f"{tag}_sum"), 1)

        def rstd_act(act, tag, sums):
            act.wait_ge(sem(f"{tag}_sum"), sums)
            nc.scalar.activation(rstd[:], ps[:, 0, :], ACT.Ln, scale=1.0 / D,
                                 bias=eps[:]).then_inc(sem(f"{tag}_rstd"), 1)
            act.wait_ge(sem(f"{tag}_rstd"), 1)
            nc.scalar.activation(rstd[:], rstd[:], ACT.Exp, scale=-0.5).then_inc(sem(f"{tag}_rstd"), 1)

        def post_act(act, tag, stage):
            last_pair = FIRST[stage] + dict(STAGES)[stage] - 1
            more = last_pair + 1 < N_PAIRS
            if more:
                head(act, last_pair, 0)
            nc.scalar.preload_act_table_set("natural_log_exp_and_others")
            for d in range(KT):
                if d < KT - 1:
                    act.wait_ge(sem(f"{stage}_bank"), d + 1)
                else:
                    act.wait_ge(block_done, 2 * (FIRST[stage] + dict(STAGES)[stage]))
                if d >= 2:
                    act.wait_ge(sem(f"{tag}_acc"), max(1, d - 2))
                nc.scalar.activation(sq[:, d % 2, :], ps[:, d, :], ACT.Square).then_inc(sem(f"{tag}_sq"), 1)
            if more:
                head(act, last_pair, 1)
            rstd_act(act, tag, 1)

        def post_dve(dve, tag, stage, gain):
            last_pair = FIRST[stage] + dict(STAGES)[stage] - 1
            more = last_pair + 1 < N_PAIRS
            if more:
                tail(dve, last_pair, 0)
            dve.wait_ge(sem(f"{tag}_sq"), 1)
            nc.vector.tensor_copy(y0[:], ps[:, 0, :]).then_inc(sem(f"{tag}_y0"), 1)
            acc_dve(dve, tag)
            if more:
                tail(dve, last_pair, 1)

            def scaled(d):
                if d == 0:
                    dve.wait_ge(sem(f"{tag}_y0"), 1)
                    dve.wait_ge(sem(f"{tag}_rstd"), 2)
                if d >= 2:
                    dve.wait_ge(sem(f"{tag}_x"), d - 1)
                nc.vector.scalar_tensor_tensor(out=tmp[:, d % 2, :], in0=y0[:] if d == 0 else ps[:, d, :],
                                               scalar=gain[:, d:d + 1], in1=rstd[:], op0=ALU.mult,
                                               op1=ALU.mult).then_inc(sem(f"{tag}_scaled"), 1)
            scaled(0)
            for d in range(KT):
                if d + 1 < KT:
                    scaled(d + 1)
                dve.wait_ge(sem(f"{tag}_scaled"), d + 1)
                nc.vector.tensor_tensor(xt[:, d, :], xt[:, d, :], tmp[:, d % 2, :],
                                        ALU.add).then_inc(sem(f"{tag}_x"), 1)

        def pre_act(act, tag, x_ready):
            for d in range(KT):
                if tag == "pre1":
                    act.wait_ge(sem(f"x_in{d // 2}"), 16)
                else:
                    act.wait_ge(x_ready, d + 1)
                if d >= 2:
                    if tag == "pre1":
                        act.wait_ge(sem(f"{tag}_acc"), max(1, d - 2))
                    else:
                        act.wait_ge(sem(f"{tag}_sum"), d - 1)
                nc.scalar.activation(sq[:, d % 2, :], xt[:, d, :], ACT.Square).then_inc(sem(f"{tag}_sq"), 1)
            rstd_act(act, tag, 1 if tag == "pre1" else KT)
            for d in range(KT):
                act.wait_ge(sem(f"{tag}_norm"), d + 1)
                nc.scalar.activation(hh[:, d, :], tmp[:, d % 2, :], ACT.Copy).then_inc(sem(f"{tag}_head"), 1)

        def pre_dve(dve, tag, gain):
            def norm(d):
                if d == 0:
                    dve.wait_ge(sem(f"{tag}_rstd"), 2)
                if d >= 2:
                    dve.wait_ge(sem(f"{tag}_ready"), d - 1)
                nc.vector.scalar_tensor_tensor(out=tmp[:, d % 2, :], in0=xt[:, d, :], scalar=gain[:, d:d + 1],
                                               in1=rstd[:], op0=ALU.mult,
                                               op1=ALU.mult).then_inc(sem(f"{tag}_norm"), 1)
            norm(0)
            for d in range(KT):
                if d + 1 < KT:
                    norm(d + 1)
                dve.wait_ge(sem(f"{tag}_head"), d + 1)
                nc.vector.tensor_tensor(hl[:, d, :], tmp[:, d % 2, :], hh[:, d, :].bitcast(F32),
                                        ALU.subtract).then_inc(sem(f"{tag}_ready"), 1)

        def tokens_pe(pe, stage, turns, strided, ready):
            first = FIRST[stage]
            with pe.Fori(0, turns) as g:
                for b in range(4):
                    pair, s = first + 2 * g + b // 2, b % 2
                    pe.wait_ge(split_done, 2 * pair + s + 1)
                    order = [(k, t) for k in range(2) for t in range(TT)] if b < 3 else \
                        [(k, t) for t in range(TT) for k in range(2)]
                    for k, t in order:
                        kt = 2 * b + k
                        if ready and t == 0:
                            pe.wait_ge(ready, kt + 1)
                        if kt == 0:
                            pe.wait_ge(sem(f"{stage}_out{t // 2}"), 2 * g + 1)
                        m = [x[:, kt, :].rearrange("p (u r) -> p r u", r=R)[:, t, :] if strided
                             else x[:, kt, t * P:(t + 1) * P] for x in (hh, hl)]
                        w = wcols(s, k * S, S)
                        nc.tensor.matmul(ps[:, t, :], m[0], w[0], start=kt == 0, stop=False)
                        nc.tensor.matmul(ps[:, t, :], m[1], w[0], start=False, stop=False)
                        last = nc.tensor.matmul(ps[:, t, :], m[0], w[1], start=False, stop=kt == KT - 1)
                        if kt == KT - 1 and t < TT - 1:
                            last.then_inc(sem(f"{stage}_bank"), 1)
                    last.then_inc(block_done, 1)

        def tokens_dst(stage, g, t):
            if stage == "v":
                return v_tok[:, bass.ds(g, 1), t, :].rearrange("p a n -> p (a n)")
            return ih_tok[:, t, bass.ds(g * S, S)]

        def tokens_act(act, stage, turns):
            first = FIRST[stage]
            with act.Fori(0, turns) as g:
                for b in range(3):
                    head(act, first + 2 * g + b // 2, b % 2)
                for t in range(2):
                    act.wait_ge(sem(f"{stage}_bank"), 3 * g + t + 1)
                    nc.scalar.activation(tokens_dst(stage, g, t), ps[:, t, :],
                                         ACT.Copy).then_inc(sem(f"{stage}_out0"), 1)
                head(act, first + 2 * g + 1, 1)

        def tokens_dve(dve, stage, turns):
            first = FIRST[stage]
            with dve.Fori(0, turns) as g:
                for b in range(3):
                    tail(dve, first + 2 * g + b // 2, b % 2)
                for t in range(2, 4):
                    if t == 2:
                        dve.wait_ge(sem(f"{stage}_bank"), 3 * g + 3)
                    else:
                        dve.wait_ge(block_done, 2 * (first + 2 * g) + 4)
                    nc.vector.tensor_copy(tokens_dst(stage, g, t), ps[:, t, :]).then_inc(sem(f"{stage}_out1"), 1)
                tail(dve, first + 2 * g + 1, 1)

        def attn_pe(pe):
            first = FIRST["qk"]
            scored, prob_done = sem("scored"), sem("prob_done")
            turned, turned_out = sem("turned"), sem("turned_out")
            summed, o_out = sem("summed"), sem("o_out")
            with pe.Fori(0, PAIRS_H) as hp:
                pe.wait_ge(o_out, 8 * hp + 1)
                for g in range(N_GROUPS):
                    pe.wait_ge(sem("q_out"), 3 * hp + g + 1)
                    project(pe, first + 3 * hp + g, 0, ps[:, 0, :], hh, hl)
                    pe.wait_ge(sem("k_out"), 3 * hp + g + 1)
                    project(pe, first + 3 * hp + g, 1, ps[:, 1, :], hh, hl)
                pe.wait_ge(sem("q_out"), 3 * hp + 4)
                pe.wait_ge(sem("k_out"), 3 * hp + 4)

                def scores(n):
                    e, r = n // R, n % R
                    rows = slice(HD * e, HD * e + HD)
                    if n >= 2:
                        pe.wait_ge(sem("biased"), 8 * hp + n - 1)
                    b = 2 + 2 * (n % 2)
                    nc.tensor.matmul(ps[:, b, :], q_t[rows, 0, r, :],
                                     k_t[rows, 0, :, :].rearrange("p r u -> p (r u)"), start=True, stop=True)
                    for g in (1, 2):
                        last = nc.tensor.matmul(ps[:, b + 1, (g - 1) * U:g * U], q_t[rows, g, r, :],
                                                k_t[rows, g, r, :], start=True, stop=True)
                    last.then_inc(scored, 1)

                scores(0)
                scores(1)
                for n in range(8):
                    pe.wait_ge(prob_done, 8 * hp + n + 1)
                    pe.wait_ge(turned_out, 8 * hp + n + 1)
                    for k in range(6):
                        last = nc.tensor.transpose(ps[:, 6 + k // 4, (k % 4) * U:(k % 4 + 1) * U],
                                                   prob[:, n % 2, k * U:(k + 1) * U], ident)
                    last.then_inc(turned, 1)
                    if n + 2 < 8:
                        scores(n + 2)
                    pe.wait_ge(turned_out, 8 * hp + n + 2)
                    if n >= 2:
                        pe.wait_ge(o_out, 8 * hp + n)
                    e, r = n // R, n % R
                    for k in range(6):
                        g, tile = (0, k) if k < R else (k - R + 1, r)
                        last = nc.tensor.matmul(ps[:, n % 2, 0:P], prob_t[:, n % 2, k * U:(k + 1) * U],
                                                v_tok[:, g, tile, bass.ds(hp * P, P)],
                                                start=k == 0, stop=k == 5)
                    last.then_inc(summed, 1)
            pe.wait_ge(o_out, 8 * PAIRS_H + 1)
            for ft in range(4):
                for r in range(R):
                    last = nc.tensor.transpose(ps[:, ft, r * U:(r + 1) * U], o_tok[:, r, ft * P:(ft + 1) * P],
                                               ident)
                last.then_inc(sem("a_turned"), 1)

        def attn_act(act):
            first = FIRST["qk"]
            nc.scalar.preload_act_table_set("natural_log_exp_and_others")
            with act.Fori(0, PAIRS_H) as hp:
                for g in range(N_GROUPS):
                    head(act, first + 3 * hp + g, 0)
                    nc.scalar.activation(q_t[:, g, :, :], ps[:, 0, :].rearrange("p (u r) -> p r u", r=R)[:, :, ::-1],
                                         ACT.Copy, scale=HD ** -0.5).then_inc(sem("q_out"), 1)
                    head(act, first + 3 * hp + g, 1)

                def softmax(n):
                    act.wait_ge(sem("maxed"), 8 * hp + n + 1)
                    nc.scalar.activation(prob[:, n % 2, :], prob[:, n % 2, :], ACT.Exp, bias=neg_max[:, n:n + 1],
                                         accum_out=row_sum[:, n:n + 1]).then_inc(sem("prob_done"), 1)

                def turned_copy(n):
                    act.wait_ge(sem("turned"), 8 * hp + n + 1)
                    act.wait_ge(sem("summed"), 8 * hp + n - 1) if n >= 2 else None
                    nc.scalar.activation(prob_t[:, n % 2, :],
                                         ps[:, 6:8, :].rearrange("p a n -> p (a n)")[:, 0:6 * U],
                                         ACT.Copy).then_inc(sem("turned_out"), 1)

                softmax(0)
                softmax(1)
                turned_copy(0)
                for n in range(1, 8):
                    turned_copy(n)
                    if n + 1 < 8:
                        softmax(n + 1)
            for ft in range(4):
                act.wait_ge(sem("a_turned"), ft + 1)
                nc.scalar.activation(ath[:, ft, :].rearrange("p (u r) -> p r u", r=R),
                                     ps[:, ft, :].rearrange("p (r u) -> p r u", r=R)[:, :, ::-1],
                                     ACT.Copy).then_inc(sem("ath_done"), 1)

        def attn_dve(dve):
            first = FIRST["qk"]
            with dve.Fori(0, PAIRS_H) as hp:
                for g in range(N_GROUPS):
                    tail(dve, first + 3 * hp + g, 0)
                    dve.wait_ge(block_done, 2 * (first + 3 * hp + g) + 2)
                    nc.vector.tensor_copy(k_t[:, g, :, :], ps[:, 1, :].rearrange("p (u r) -> p r u", r=R)
                                          ).then_inc(sem("k_out"), 1)
                    tail(dve, first + 3 * hp + g, 1)
                dve.wait_ge(sem("bias_in"), 32 * hp + 32)

                def biased(n):
                    e, r = n // R, n % R
                    dve.wait_ge(sem("scored"), 8 * hp + n + 1)
                    if n >= 2:
                        dve.wait_ge(sem("turned"), 8 * hp + n - 1)
                    b = 2 + 2 * (n % 2)
                    nc.vector.tensor_tensor(prob[:, n % 2, 0:S], ps[:, b, :],
                                            bias[:, e, R - 1 - r:2 * R - 1 - r, :].rearrange("p c u -> p (c u)"),
                                            ALU.add).then_inc(sem("biased_0"), 1)
                    nc.vector.tensor_tensor(prob[:, n % 2, S:6 * U], ps[:, b + 1, 0:2 * U],
                                            bias[:, e, N_TAB - 2:N_TAB, :].rearrange("p c u -> p (c u)"),
                                            ALU.add).then_inc(sem("biased"), 1)
                    dve.wait_ge(sem("biased_0"), 8 * hp + n + 1)
                    dve.wait_ge(sem("biased"), 8 * hp + n + 1)
                    nc.vector.tensor_reduce(neg_max[:, n:n + 1], prob[:, n % 2, :], AXIS_X, ALU.max,
                                            negate=True).then_inc(sem("maxed"), 1)

                def outputs(n):
                    e, r = n // R, n % R
                    dve.wait_ge(sem("prob_done"), 8 * hp + n + 1)
                    nc.vector.reciprocal(row_inv[:, n:n + 1], row_sum[:, n:n + 1]).then_inc(sem("inverted"), 1)
                    dve.wait_ge(sem("inverted"), 8 * hp + n + 1)
                    dve.wait_ge(sem("summed"), 8 * hp + n + 1)
                    nc.vector.tensor_scalar(o_tok[:, r, bass.ds(hp * 2 * HD + e * HD, HD)], ps[:, n % 2, e * HD:(e + 1) * HD],
                                            row_inv[:, n:n + 1], None, ALU.mult).then_inc(sem("o_out"), 1)

                biased(0)
                biased(1)
                for n in range(8):
                    if n + 2 < 8:
                        biased(n + 2)
                    outputs(n)
            for ft in range(4):
                dve.wait_ge(sem("ath_done"), ft + 1)
                nc.vector.tensor_tensor(atl[:, ft, :].rearrange("p (u r) -> p r u", r=R),
                                        ps[:, ft, :].rearrange("p (r u) -> p r u", r=R)[:, :, ::-1],
                                        ath[:, ft, :].rearrange("p (u r) -> p r u", r=R).bitcast(F32),
                                        ALU.subtract).then_inc(sem("atl_done"), 1)

        def gate_a_pe(pe):
            first = FIRST["gate_a"]
            pe.wait_ge(sem("atl_done"), 4)
            with pe.Fori(0, 2) as i:
                for m in range(4):
                    pe.wait_ge(sem("sig_a_done"), 4 * i + 1)
                    project(pe, first + 3 * i + m // 2, m % 2, ps[:, m, :], hh, hl)
                for b in range(2):
                    pair = first + 3 * i + 2
                    pe.wait_ge(split_done, 2 * pair + b + 1)
                    for d in range(2):
                        m = 2 * b + d
                        pe.wait_ge(sem("y_a"), 4 * i + 1)
                        for kt in range(4):
                            last = product(ps[:, 4 + m, :], *wcols(b, d * S + kt * P), ath[:, kt, :],
                                           atl[:, kt, :], kt == 0, kt == 3)
                    last.then_inc(block_done, 1)

        def gate_a_act(act):
            first = FIRST["gate_a"]
            nc.scalar.preload_act_table(ACT.Sigmoid)
            with act.Fori(0, 2) as i:
                for m in range(4):
                    head(act, first + 3 * i + m // 2, m % 2)
                    act.wait_ge(sem("y_a"), 4 * i + 1)
                    nc.scalar.activation(sig_a[:, m, :], ps[:, m, :], ACT.Sigmoid).then_inc(sem("sig_a_done"), 1)
                for b in range(2):
                    head(act, first + 3 * i + 2, b)

        def gate_a_dve(dve):
            first = FIRST["gate_a"]
            with dve.Fori(0, 2) as i:
                for m in range(4):
                    tail(dve, first + 3 * i + m // 2, m % 2)
                for b in range(2):
                    tail(dve, first + 3 * i + 2, b)
                    for m in (2 * b, 2 * b + 1):
                        dve.wait_ge(sem("sig_a_done"), 4 * i + m + 2)
                        nc.vector.tensor_tensor(ymix[:, bass.ds(4 * i + m, 1), :].rearrange("p a n -> p (a n)"),
                                                sig_a[:, m, :], ps[:, 4 + m, :], ALU.mult).then_inc(sem("y_a"), 1)

        def both(x):
            return x.rearrange("p (n c) -> p n c", c=C)

        REF = (C // 2, C // 2 - 1)
        END = (C - 1, 0)

        def hgrn_pe(pe):
            first = FIRST["hgrn"]

            def turn(h, proj, scan):
                def project_part(b, free):
                    if proj:
                        if free:
                            pe.wait_ge(sem(free[0]), free[1])
                        project(pe, first + 2 * h + b // 2, b % 2, ps[:, b % 2, :], hh, hl)

                project_part(0, ("sig_f1", h) if scan else None)
                if scan:
                    for d in range(2):
                        pe.wait_ge(sem(f"k_end{d}"), h)
                        for t in range(TT):
                            last = nc.tensor.transpose(ps[:, 2 + d, t * P:(t + 1) * P],
                                                       e_dn[d][:, t * P:(t + 1) * P], ident)
                        last.then_inc(sem(f"kh_turned{d}"), 1)
                    for d in range(2):
                        pe.wait_ge(sem(f"q_st{d}"), h)
                        if d:
                            pe.wait_ge(sem("b_done"), h)
                        for t in range(TT):
                            cols = slice(t * P, (t + 1) * P)
                            last = nc.tensor.matmul(ps[:, 4 + d, cols], k_in[d][:, cols], q_in[d][:, cols],
                                                    start=True, stop=True)
                        last.then_inc(sem(f"att_psum{d}"), 1)
                project_part(1, ("gate_done", h) if scan else None)
                if scan:
                    pe.wait_ge(sem("v_taken"), h)
                    for d in range(2):
                        pe.wait_ge(sem("kh_out1"), h)
                        for i in range(NC_CH - 1):
                            n = i if d == 0 else NC_CH - 1 - i
                            rows = slice(C * (n % 2), C * (n % 2) + C)
                            nc.tensor.matmul(ps[:, (6, 2)[d] + n % 2, (n // 2) * P:(n // 2 + 1) * P],
                                             kh_tok[d][rows, n // 2, :], v_h[rows, n // 2, :],
                                             start=True, stop=True).then_inc(sem(f"added{d}"), 1)
                project_part(2, ("sig_q" if h is GH_HEADS else "q_done", h + 1))
                if scan:
                    for d in range(2):
                        pe.wait_ge(sem(f"att_out{d}"), h)
                        pe.wait_ge(sem(f"state{d}"), (NC_CH - 1) * h)
                    for t in range(TT):
                        out = ps[:, 4, t * P:(t + 1) * P]
                        nc.tensor.matmul(out, att[0][:, t, :], v_h[:, t, :], start=True, stop=False)
                        nc.tensor.matmul(out, att[1][:, t, :], v_h[:, t, :], start=False, stop=False)
                        for half in range(2):
                            n = 2 * t + half
                            part = ps[C * half:C * half + C, 4, t * P:(t + 1) * P]
                            dirs = [d for d in range(2) if n != (0, NC_CH - 1)[d]]
                            for d in dirs:
                                i = (n - 1, NC_CH - 2 - n)[d]
                                last = nc.tensor.matmul(part, q_st[d][:, n * C:(n + 1) * C], state[d][:, i, :],
                                                        start=False, stop=d == dirs[-1])
                    last.then_inc(sem("o_psum"), 1)
                project_part(3, ("sig_f0", h + 1))
                if scan:
                    pe.wait_ge(sem("o_norm"), TT * h)
                    for t in range(TT):
                        last = nc.tensor.transpose(ps[:, 5, t * P:(t + 1) * P], o_nrm[:, t, :], ident)
                    last.then_inc(sem("o_turned"), 1)

            turn(0, True, False)
            with pe.Fori(1, GH_HEADS) as h:
                turn(h, True, True)
            turn(GH_HEADS, True, True)

        def hgrn_act(act):
            first = FIRST["hgrn"]

            def turn(h, proj, scan):
                own = h is not GH_HEADS
                if proj:
                    head(act, first + 2 * h, 0)
                    nc.scalar.activation(sig_q, ps[:, 0, :], ACT.Sigmoid).then_inc(sem("sig_q"), 1)
                if scan:
                    for d in range(2):
                        act.wait_ge(sem(f"kh_turned{d}"), h)
                        nc.scalar.activation(kh_tok[d][:].rearrange("p t k -> p (t k)"), ps[:, 2 + d, :],
                                             ACT.Copy).then_inc(sem(f"kh_out{d}"), 1)
                if proj:
                    head(act, first + 2 * h, 1)
                    nc.scalar.activation(sig[0][:], ps[:, 1, :], ACT.Sigmoid).then_inc(sem("sig_f0"), 1)
                    head(act, first + 2 * h + 1, 0)
                    nc.scalar.activation(sig[1][:], ps[:, 0, :], ACT.Sigmoid).then_inc(sem("sig_f1"), 1)
                if own:
                    for d in range(2):
                        lane = bass.ds(d * GH_HEADS + h, 1)
                        act.wait_ge(sem(f"sig_f{d}"), h + 1)
                        nc.scalar.activation(cum[d][:], sig[d][:], ACT.Ln, scale=oml[:, lane],
                                             bias=lb[:, lane]).then_inc(sem(f"logf{d}"), 1)
                if scan:
                    act.wait_ge(sem("o_psum"), h + 1)
                    for t in range(TT):
                        nc.scalar.activation(o_nrm[:, t, :], ps[:, 4, t * P:(t + 1) * P], ACT.Square,
                                             accum_out=o_ss[:, t:t + 1]).then_inc(sem("o_ss"), 1)
                    act.wait_ge(sem("o_ss"), TT * h)
                    nc.scalar.activation(o_rs[:], o_ss[:], ACT.Ln, scale=1.0 / P,
                                         bias=eps[:]).then_inc(sem("o_ln"), 1)
                    act.wait_ge(sem("o_ln"), h)
                    nc.scalar.activation(o_rs[:], o_rs[:], ACT.Exp, scale=-0.5).then_inc(sem("o_rstd"), 1)
                if own:
                    for d in range(2):
                        act.wait_ge(sem(f"cum{d}"), h + 1)
                        nc.scalar.activation(e_ref[d][:], both(cum[d][:])[:, :, REF[d]], ACT.Exp
                                             ).then_inc(sem(f"e_ref{d}"), 1)
                        nc.scalar.activation(decay[d][:], both(cum[d][:])[:, :, END[d]], ACT.Exp
                                             ).then_inc(sem(f"decay{d}"), 1)
                        act.wait_ge(sem(f"rel{d}"), h + 1)
                        nc.scalar.activation(e_up[d][:], k_in[d][:], ACT.Exp).then_inc(sem(f"e_up{d}"), 1)
                        nc.scalar.activation(e_dn[d][:], k_in[d][:], ACT.Exp,
                                             scale=-1.0).then_inc(sem(f"e_dn{d}"), 1)
                if proj:
                    head(act, first + 2 * h + 1, 1)
                    nc.scalar.activation(sig_g, ps[:, 1, :], ACT.Sigmoid).then_inc(sem("sig_g"), 1)
                if scan:
                    act.wait_ge(sem("b_done"), h + 1)
                    nc.scalar.activation(bh[:, bass.ds(h - 1, 1), :].rearrange("p a n -> p (a n)"), b_out,
                                         ACT.Copy).then_inc(sem("bh_done"), 1)

            turn(0, True, False)
            with act.Fori(1, GH_HEADS) as h:
                turn(h, True, True)
            turn(GH_HEADS, True, True)

        def hgrn_dve(dve):
            first = FIRST["hgrn"]
            for d in range(2):
                nc.vector.memset(att[d][:], 0.0).then_inc(sem("att_zero"), 1)
            dve.wait_ge(sem("att_zero"), 2)

            def products(h, d):
                dve.wait_ge(sem(f"e_up{d}"), h + 1)
                nc.vector.tensor_tensor(q_in[d][:], q_h[:], e_up[d][:], ALU.mult).then_inc(sem(f"q_in{d}"), 1)
                dve.wait_ge(sem(f"e_dn{d}"), h + 1)
                nc.vector.tensor_tensor(k_in[d][:], key[d][:], e_dn[d][:], ALU.mult).then_inc(sem(f"k_in{d}"), 1)
                dve.wait_ge(sem(f"k_in{d}"), h + 1)
                nc.vector.tensor_tensor(both(e_dn[d][:]), both(k_in[d][:]),
                                        both(e_up[d][:])[:, :, END[d]:END[d] + 1].to_broadcast([P, NC_CH, C]),
                                        ALU.mult).then_inc(sem(f"k_end{d}"), 1)
                dve.wait_ge(sem(f"q_in{d}"), h + 1)
                dve.wait_ge(sem(f"e_ref{d}"), h + 1)
                nc.vector.tensor_tensor(both(q_st[d][:]), both(q_in[d][:]),
                                        e_ref[d][:].unsqueeze(2).to_broadcast([P, NC_CH, C]),
                                        ALU.mult).then_inc(sem(f"q_st{d}"), 1)

            def turn(h, proj, scan):
                own = h is not GH_HEADS
                if proj:
                    tail(dve, first + 2 * h, 0)
                if own:
                    dve.wait_ge(sem("sig_q"), h + 1)
                    nc.vector.tensor_tensor(q_h[:], sig_q, ps[:, 0, :], ALU.mult).then_inc(sem("q_done"), 1)
                if scan:
                    for d in range(2):
                        dve.wait_ge(sem(f"att_psum{d}"), h)
                        nc.vector.tensor_copy(wait_taker[:, d:d + 1], eps[:])
                        nc.vector.copy_predicated(att[d][:],
                                                  tri[d].unsqueeze(1).to_broadcast([P, TT, P]).bitcast(U32),
                                                  ps[:, 4 + d, :].rearrange("p (t c) -> p t c", c=P)
                                                  ).then_inc(sem(f"att_out{d}"), 1)
                if proj:
                    tail(dve, first + 2 * h, 1)
                if scan:
                    for i in range(NC_CH - 1):
                        for d in range(2):
                            n = i if d == 0 else NC_CH - 1 - i
                            if i == 0:
                                dve.wait_ge(sem(f"added{d}"), (NC_CH - 1) * h)
                            new = ps[:, (6, 2)[d] + n % 2, (n // 2) * P:(n // 2 + 1) * P]
                            if i == 0:
                                nc.vector.tensor_copy(state[d][:, 0, :], new).then_inc(sem(f"state{d}"), 1)
                            else:
                                if i == 1:
                                    dve.wait_ge(sem(f"decay{d}"), h)
                                dve.wait_ge(sem(f"state{d}"), (NC_CH - 1) * (h - 1) + i)
                                nc.vector.scalar_tensor_tensor(out=state[d][:, i, :], in0=state[d][:, i - 1, :],
                                                               scalar=decay[d][:, n:n + 1], in1=new,
                                                               op0=ALU.mult, op1=ALU.add
                                                               ).then_inc(sem(f"state{d}"), 1)
                if proj:
                    tail(dve, first + 2 * h + 1, 0)
                if own:
                    for d in range(2):
                        flip = slice(None, None, -1) if d else slice(None)
                        lane = bass.ds(d * GH_HEADS + h, 1)
                        dve.wait_ge(sem(f"logf{d}"), h + 1)
                        nc.vector.tensor_tensor_scan(out=cum[d][:, flip], data0=keep_state[d][:, flip],
                                                     data1=cum[d][:, flip], initial=0.0, op0=ALU.mult,
                                                     op1=ALU.add).then_inc(sem(f"cum{d}"), 1)
                        nc.vector.tensor_scalar(sig[d][:], sig[d][:], -1.0, 1.0, ALU.mult,
                                                ALU.add).then_inc(sem(f"one_less{d}"), 1)
                        dve.wait_ge(sem(f"cum{d}"), h + 1)
                        nc.vector.tensor_tensor(both(k_in[d][:]), both(cum[d][:]),
                                                both(cum[d][:])[:, :, REF[d]:REF[d] + 1
                                                                ].to_broadcast([P, NC_CH, C]),
                                                ALU.subtract).then_inc(sem(f"rel{d}"), 1)
                        dve.wait_ge(sem(f"one_less{d}"), h + 1)
                        nc.vector.tensor_scalar(key[d][:], sig[d][:], oml[:, lane], None,
                                                ALU.mult).then_inc(sem(f"key{d}"), 1)
                if scan:
                    dve.wait_ge(sem("o_rstd"), h)
                    for t in range(TT):
                        nc.vector.tensor_scalar(o_nrm[:, t, :], ps[:, 4, t * P:(t + 1) * P], o_rs[:, t:t + 1],
                                                None, ALU.mult).then_inc(sem("o_norm"), 1)
                if own:
                    dve.wait_ge(sem("q_done"), h + 1)
                    dve.wait_ge(sem("key1"), h + 1)
                    products(h, 0)
                if proj:
                    tail(dve, first + 2 * h + 1, 1)
                if own:
                    products(h, 1)
                if scan:
                    dve.wait_ge(sem("o_turned"), h)
                    nc.vector.tensor_tensor(b_out, gate[:], ps[:, 5, :], ALU.mult).then_inc(sem("b_done"), 1)
                if own:
                    if scan:
                        dve.wait_ge(sem("b_done"), h + 1)
                    dve.wait_ge(sem("sig_g"), h + 1)
                    nc.vector.scalar_tensor_tensor(out=gate[:], in0=ps[:, 1, :], scalar=par[:, 48:49], in1=sig_g,
                                                   op0=ALU.mult, op1=ALU.mult).then_inc(sem("gate_done"), 1)
                if scan:
                    dve.wait_ge(sem("bh_done"), h)
                    one = bass.ds(h - 1, 1)
                    nc.vector.tensor_tensor(bl[:, one, :].rearrange("p a n -> p (a n)"), b_out,
                                            bh[:, one, :].rearrange("p a n -> p (a n)").bitcast(F32),
                                            ALU.subtract).then_inc(sem("bl_done"), 1)

            turn(0, True, False)
            with dve.Fori(1, GH_HEADS) as h:
                turn(h, True, True)
            turn(GH_HEADS, True, True)

        def gate_h_pe(pe):
            first = FIRST["gate_h"]
            pe.wait_ge(sem("bl_done"), GH_HEADS)
            for d in range(4):
                project(pe, first + d // 2, d % 2, ps[:, 2 + d, :], bh, bl)
            pe.wait_ge(sem("sig_g"), GH_HEADS + 1)
            with pe.Fori(4, KT) as d:
                pe.wait_ge(sem("sig_h_done"), d - 3)
                project(pe, first + d - 2, 0, ps[:, 0, :], hh, hl)
                pe.wait_ge(sem("y_h"), d + 1)
                project(pe, first + d - 2, 1, ps[:, 1, :], bh, bl)

        def gate_h_act(act):
            first = FIRST["gate_h"]

            def y_head(d):
                one = bass.ds(d, 1)
                act.wait_ge(sem("y_sum"), d + 2)
                nc.scalar.activation(yh[:, one, :].rearrange("p a n -> p (a n)"),
                                     ymix[:, one, :].rearrange("p a n -> p (a n)"),
                                     ACT.Copy).then_inc(sem("yh_done"), 1)

            for d in range(4):
                head(act, first + d // 2, d % 2)
                y_head(d)
            with act.Fori(4, KT) as d:
                head(act, first + d - 2, 0)
                act.wait_ge(sem("y_h"), d + 1)
                nc.scalar.activation(sig_h[:], ps[:, 0, :], ACT.Sigmoid).then_inc(sem("sig_h_done"), 1)
                head(act, first + d - 2, 1)
                y_head(d)

        def gate_h_dve(dve):
            first = FIRST["gate_h"]

            def y_step(d, gated, product, gate_tail):
                one = bass.ds(d, 1)
                y = ymix[:, one, :].rearrange("p a n -> p (a n)")
                nc.vector.tensor_tensor(gated[0], gated[1], product, ALU.mult).then_inc(sem("y_h"), 1)
                dve.wait_ge(sem("y_h"), d + 2)
                nc.vector.tensor_tensor(y, y, gated[0], ALU.add).then_inc(sem("y_sum"), 1)
                tail(dve, *gate_tail)
                dve.wait_ge(sem("yh_done"), d + 1)
                nc.vector.tensor_tensor(yl[:, one, :].rearrange("p a n -> p (a n)"), y,
                                        yh[:, one, :].rearrange("p a n -> p (a n)").bitcast(F32),
                                        ALU.subtract).then_inc(sem("yl_done"), 1)

            for d in range(4):
                dve.wait_ge(block_done, 2 * first + d + 1)
                if d == 0:
                    dve.wait_ge(sem("sig_g"), GH_HEADS + 1)
                y_step(d, (first_gates[d], first_gates[d]), ps[:, 2 + d, :], (first + d // 2, d % 2))
            with dve.Fori(4, KT) as d:
                tail(dve, first + d - 2, 0)
                dve.wait_ge(sem("sig_h_done"), d - 2)
                dve.wait_ge(block_done, 2 * (first + d - 2) + 2)
                dve.wait_ge(sem("y_sum"), d + 1)
                y_step(d, (tmp[:, 0, :], sig_h[:]), ps[:, 1, :], (first + d - 2, 1))

        block = ctx.enter_context(nc.Block())

        @block.sync
        def _(sp):
            for i in range(X_PARTS):
                sp.dma_start(xt[:, 2 * i:2 * i + 2, :], x_t[2 * i * P:(2 * i + 2) * P, :].rearrange(
                    "(d p) n -> p d n", p=P)).then_inc(sem(f"x_in{i}"), 16)
            for s in range(2):
                sp.dma_start(raw[:, s, :], wstream[s]).then_inc(raw_in[s], 16)
            with sp.Fori(1, N_PAIRS) as pair:
                load_block(sp, pair, 0)
                load_block(sp, pair, 1)
            for d in range(KT):
                sp.wait_ge(sem("post3_x"), d + 1)
                sp.dma_start(out_t[d * P:(d + 1) * P, :], xt[:, d, :]).then_inc(sem("stored"), 16)
            sp.wait_ge(sem("stored"), 16 * KT)

        @block.gpsimd
        def _(pool):
            pool.dma_start(par[:], params).then_inc(sem("par_in"), 16)
            for i in range(X_PARTS):
                pool.wait_ge(sem(f"x_in{i}"), 16)
            pool.dma_start(table[0:BUCKETS, :], rel_bias).then_inc(sem("table_in"), 16)
            pool.dma_start(hot_sb[:], onehot).then_inc(sem("hot_in"), 16)
            pool.dma_start(cst[:], consts).then_inc(sem("cst_in"), 16)
            pool.wait_ge(sem("vec_out"), 1)
            pool.dma_start(vec_dram.ap().rearrange("h c m -> h (c m)"), vec_sb[:]).then_inc(sem("vec_stored"), 16)
            pool.wait_ge(sem("vec_stored"), 16)
            for hp in range(PAIRS_H):
                if hp == 0:
                    pool.wait_ge(sem("post1_x"), KT)
                else:
                    pool.wait_ge(sem("biased"), 8 * hp)
                for e in range(2):
                    src = bass.AP(tensor=vec_dram, offset=(2 * hp + e) * N_TAB * VEC,
                                  ap=[[1, U], [VEC, N_TAB], [1, U]])
                    pool.dma_start(bias[:, e, :, :], src).then_inc(sem("bias_in"), 16)
            with pool.Fori(0, GH_HEADS) as h:
                pool.wait_ge(sem("ih_out0"), 5)
                pool.wait_ge(sem("ih_out1"), 5)
                pool.wait_ge(sem("o_psum"), h + 1)
                nc.gpsimd.tensor_copy(v_h, ih_tok[:, :, bass.ds(h * P, P)]).then_inc(sem("v_taken"), 1)

        @block.tensor
        def _(pe):
            seed(pe, "o_psum")
            pe.wait_ge(sem("filled"), 2)
            sum_acc_pe(pe, "pre1")
            pe.wait_ge(sem("pre1_rstd"), 1)
            ffn_in_pe(pe, 1)
            pe.wait_ge(sem("glu1"), FT + 1)
            rows_pe(pe, "ffn1_out", ah, al, sem("a_tail1"), 1)
            pe.wait_ge(sem("post1_y0"), 1)
            sum_acc_pe(pe, "post1")
            pe.wait_ge(sem("post1_rstd"), 1)
            sum_pe(pe, "pre2")
            pe.wait_ge(sem("post1_scaled"), KT)
            tokens_pe(pe, "v", N_GROUPS, True, sem("pre2_ready"))
            pe.wait_ge(sem("v_out0"), 2 * N_GROUPS + 1)
            pe.wait_ge(sem("v_out1"), 2 * N_GROUPS + 1)
            pe.wait_ge(sem("cst_in"), 16)
            attn_pe(pe)
            gate_a_pe(pe)
            pe.wait_ge(sem("y_a"), 9)
            tokens_pe(pe, "ih", 2, False, None)
            pe.wait_ge(sem("ih_out0"), 5)
            pe.wait_ge(sem("ih_out1"), 5)
            hgrn_pe(pe)
            gate_h_pe(pe)
            pe.wait_ge(sem("y_h"), KT + 1)
            rows_pe(pe, "w_out", yh, yl, sem("yl_done"), 0)
            pe.wait_ge(sem("post2_y0"), 1)
            sum_acc_pe(pe, "post2")
            pe.wait_ge(sem("post2_rstd"), 1)
            sum_pe(pe, "pre3")
            pe.wait_ge(sem("pre3_rstd"), 1)
            pe.wait_ge(sem("post2_scaled"), KT)
            ffn_in_pe(pe, 3)
            pe.wait_ge(sem("glu3"), FT + 1)
            rows_pe(pe, "ffn3_out", ah, al, sem("a_tail3"), 1)
            pe.wait_ge(sem("post3_y0"), 1)
            sum_acc_pe(pe, "post3")

        @block.scalar
        def _(act):
            nc.scalar.preload_act_table_set("natural_log_exp_and_others")
            seed(act, "silu1", "silu3", "v_out0", "ih_out0", "q_out", "turned_out", "sig_a_done", "sig_h_done")
            act.wait_ge(sem("lb_step"), 3)
            nc.scalar.activation(lb_e[:], lb_e[:], ACT.Exp).then_inc(sem("lb_exp"), 1)
            act.wait_ge(sem("filled"), 3)
            pre_act(act, "pre1", None)
            ffn_in_act(act, 1)
            split_act(act, "ffn1_out", last=1)
            post_act(act, "post1", "ffn1_out")
            pre_act(act, "pre2", sem("post1_x"))
            tokens_act(act, "v", N_GROUPS)
            attn_act(act)
            gate_a_act(act)
            tokens_act(act, "ih", 2)
            hgrn_act(act)
            gate_h_act(act)
            split_act(act, "w_out", last=1)
            post_act(act, "post2", "w_out")
            pre_act(act, "pre3", sem("post2_x"))
            ffn_in_act(act, 3)
            split_act(act, "ffn3_out", last=1)
            post_act(act, "post3", "ffn3_out")

        @block.vector
        def _(dve):
            seed(dve, "glu1", "a_tail1", "glu3", "a_tail3", "v_out1", "ih_out1", "k_out", "o_out", "y_a", "b_done",
                 "y_h", "y_sum")
            dve.memset(table[BUCKETS:BUCKETS + 1, :], NEG_INF).then_inc(sem("filled"), 1)
            dve.memset(ones[:], 1.0).then_inc(sem("filled"), 1)
            dve.memset(eps[:], EPS).then_inc(sem("filled"), 1)
            dve.wait_ge(sem("par_in"), 16)
            for i, c0 in enumerate((8, 40)):
                nc.vector.tensor_scalar(half_gain[:, i, :], par[:, c0:c0 + KT], 0.5, None, ALU.mult
                                        ).then_inc(sem("half_set"), 1)
            z = par[:, 49:81].rearrange("p (d l h) -> p l d h", d=2, l=2)
            two = "p (d h) -> p d h"
            nc.vector.tensor_tensor(lb_m[:].rearrange(two, d=2), z[:, 0], z[:, 1], ALU.max).then_inc(sem("lb_step"), 1)
            dve.wait_ge(sem("lb_step"), 1)
            for l in range(2):
                nc.vector.tensor_tensor(lb_e[:, l, :].rearrange(two, d=2), z[:, l], lb_m[:].rearrange(two, d=2),
                                        ALU.subtract).then_inc(sem("lb_step"), 1)
            dve.wait_ge(sem("lb_exp"), 1)
            nc.vector.tensor_tensor(lb_s[:], lb_e[:, 0, :], lb_e[:, 1, :], ALU.add).then_inc(sem("lb_step"), 1)
            dve.wait_ge(sem("lb_step"), 4)
            nc.vector.reciprocal(lb_r[:], lb_s[:]).then_inc(sem("lb_step"), 1)
            dve.wait_ge(sem("lb_step"), 5)
            nc.vector.tensor_tensor(lb[:], lb_e[:, 0, :], lb_r[:], ALU.mult).then_inc(sem("lb_step"), 1)
            dve.wait_ge(sem("lb_step"), 6)
            nc.vector.tensor_scalar(oml[:], lb[:], -1.0, 1.0, ALU.mult, ALU.add).then_inc(sem("lb_step"), 1)
            acc_dve(dve, "pre1")
            for s in range(2):
                dve.wait_ge(raw_in[s], 16)
                nc.vector.tensor_copy(whi[:, s, :], raw[:, s, :]).then_inc(head_done, 1)
            for s in range(2):
                dve.wait_ge(head_done, s + 1)
                nc.vector.tensor_tensor(wlo[:, s, :], raw[:, s, :], whi[:, s, :].bitcast(F32),
                                        ALU.subtract).then_inc(split_done, 1)
            dve.wait_ge(sem("half_set"), 2)
            pre_dve(dve, "pre1", par[:, 0:KT])
            dve.wait_ge(sem("pre1_ready"), KT)
            ffn_in_dve(dve, 1)
            split_dve(dve, "ffn1_out", last=1)
            dve.wait_ge(sem("a_tail1"), FT + 1)
            post_dve(dve, "post1", "ffn1_out", half_gain[:, 0, :])
            dve.wait_ge(sem("post1_x"), KT)
            pre_dve(dve, "pre2", par[:, 16:16 + KT])
            tokens_dve(dve, "v", N_GROUPS)
            attn_dve(dve)
            gate_a_dve(dve)
            tokens_dve(dve, "ih", 2)
            hgrn_dve(dve)
            gate_h_dve(dve)
            split_dve(dve, "w_out", last=1)
            dve.wait_ge(sem("y_sum"), KT + 1)
            post_dve(dve, "post2", "w_out", par[:, 24:24 + KT])
            dve.wait_ge(sem("post2_x"), KT)
            pre_dve(dve, "pre3", par[:, 32:32 + KT])
            dve.wait_ge(sem("pre3_ready"), KT)
            ffn_in_dve(dve, 3)
            split_dve(dve, "ffn3_out", last=1)
            dve.wait_ge(sem("a_tail3"), FT + 1)
            post_dve(dve, "post3", "ffn3_out", half_gain[:, 1, :])


def stream(w):
    out = np.empty((2 * N_PAIRS, P, BLK), np.float32)
    n = [0]

    def put(block):
        out[n[0]] = block.reshape(P, BLK)
        n[0] += 1

    def columns(a, c0):
        put(a[:, c0:c0 + P].reshape(KT, P, P).transpose(1, 0, 2))

    def wide(a, c0):
        for b in range(4):
            put(a[2 * b * P:(2 * b + 2) * P, c0:c0 + S].reshape(2, P, S).transpose(1, 0, 2))

    def rows(a):
        for f in range(a.shape[0] // P):
            put(a[f * P:(f + 1) * P])

    def ffn(win, wout):
        for j in range(FT):
            columns(win, j * P)
            columns(win, FF + j * P)
        rows(wout)

    w_in = w["w_in"][0]
    aw = N_GROUPS * N_HEADS * HD
    qa, ka, va = 0, aw, 2 * aw
    qh, fzf, fzb, ih, gh, gate_a, gate_h = (3 * aw + i * D for i in range(7))
    ffn(w["w_ffn1_in"][0], w["w_ffn1_out"][0])
    for g in range(N_GROUPS):
        wide(w_in, va + g * N_HEADS * HD)
    for hp in range(PAIRS_H):
        for g in range(N_GROUPS):
            columns(w_in, qa + g * N_HEADS * HD + hp * P)
            columns(w_in, ka + g * N_HEADS * HD + hp * P)
    pa = w["w_proj_attn"][0].reshape(4, P, D)
    for i in range(2):
        for m in range(4):
            columns(w_in, gate_a + (4 * i + m) * P)
        for b in range(2):
            d0 = (4 * i + 2 * b) * P
            put(pa[:, :, d0:d0 + 2 * P].reshape(4, P, 2, P).transpose(1, 2, 0, 3))
    for g in range(2):
        wide(w_in, ih + g * S)
    for h in range(GH_HEADS):
        for c0 in (qh, fzf, fzb, gh):
            columns(w_in, c0 + h * P)
    for d in range(4):
        columns(w_in, gate_h + d * P)
    for d in range(4):
        columns(w["w_proj_hgrn"][0], d * P)
    for d in range(4, KT):
        columns(w_in, gate_h + d * P)
        columns(w["w_proj_hgrn"][0], d * P)
    rows(w["w_out"][0])
    ffn(w["w_ffn2_in"][0], w["w_ffn2_out"][0])
    return out


def kernel(**inputs):
    import concourse.bacc as bacc
    from concourse.bass_utils import run_bass_kernel_spmd

    w = {k: np.asarray(v) for k, v in inputs.items()}
    by_tile = [w[k][0].reshape(KT, P).T for k in ("ffn1_pre_norm", "ffn1_post_norm", "mix_pre_norm",
                                                  "mix_post_norm", "ffn2_pre_norm", "ffn2_post_norm")]
    lb = w["hgrn_lb"].reshape(2, 2, GH_HEADS, P).transpose(3, 0, 1, 2).reshape(P, 32)
    arrays = {
        "wstream": stream(w),
        "x_t": np.ascontiguousarray(w["x"][0].T),
        "params": np.ascontiguousarray(np.concatenate([*by_tile, w["hgrn_norm"][0][:, None], lb], axis=1)),
        "rel_bias": np.ascontiguousarray(w["rel_bias"]),
        "onehot": bias_buckets(),
        "consts": constants(),
    }
    nc = bacc.Bacc("TRN2", target_bir_lowering=False, num_devices=1)
    args = [nc.dram_tensor(f"in_{k}", a.shape, mybir.dt.from_np(a.dtype), kind="ExternalInput").ap()
            for k, a in arrays.items()]
    args.append(nc.dram_tensor("out_t", (D, S), F32, kind="ExternalOutput").ap())
    build(nc, *args)
    r = run_bass_kernel_spmd(nc, [{f"in_{k}": a for k, a in arrays.items()}], core_ids=[0])
    return np.ascontiguousarray(r.results[0]["out_t"].T)[None]
```
